# Optimizing a Trainium2 kernel written in Bass

```python
import jax
import jax.numpy as jnp
from jax import lax
import numpy as np

D_MODEL = 1024
BATCH = 1
SEQ = 256
DEPTH = 2

HEAD_DIM = 64
N_GROUP_HEADS = D_MODEL // (4 * HEAD_DIM)
N_SB_HEADS = N_GROUP_HEADS
N_GLA_HEADS = N_GROUP_HEADS
N_DIL_HEADS = N_GROUP_HEADS
N_FOX_HEADS = N_GROUP_HEADS
N_MIX_HEADS = N_SB_HEADS + N_GLA_HEADS + N_DIL_HEADS + N_FOX_HEADS
GLA_KEY_DIM = HEAD_DIM // 2
GLA_GATE_RANK = 16
GLA_GATE_TAU = 16.0
GLA_CHUNK = 16
DIL_PAIRS = ((128, 1), (512, 4), (2048, 16))
DIL_BLOCK = 128
Q_BLOCK = 128
PEER_HEADS = 8
PEER_N_KEYS = 128
PEER_N_EXPERTS = PEER_N_KEYS * PEER_N_KEYS
PEER_QUERY_DIM = 256
PEER_TOPK = 16
PEER_TOKEN_BLOCK = 128
NORM_EPS = 1e-6

GROUP_W = N_GROUP_HEADS * HEAD_DIM
GLA_QK_W = N_GLA_HEADS * GLA_KEY_DIM
IN_SPLITS = (GROUP_W, GROUP_W, GROUP_W,
             GLA_QK_W, GLA_QK_W, GROUP_W, GROUP_W, GLA_GATE_RANK,
             GROUP_W, GROUP_W, GROUP_W,
             GROUP_W, GROUP_W, GROUP_W, N_FOX_HEADS)
PROJ_W = sum(IN_SPLITS)

kernel_name = 'hybrid_sb_gla_dilated_fox_peer_trunk'

def rms_norm(x, g):
    xf = x.astype(jnp.float32)
    y = xf * lax.rsqrt(jnp.mean(xf * xf, axis=-1, keepdims=True) + NORM_EPS)
    return (y * g.astype(jnp.float32)).astype(x.dtype)

def head_rms_norm(o, g):
    of = o.astype(jnp.float32)
    y = of * lax.rsqrt(jnp.mean(of * of, axis=-1, keepdims=True) + NORM_EPS)
    return y * g.astype(jnp.float32)[None, :, None, :]

def to_heads(t, n):
    b, s, _ = t.shape
    return t.reshape(b, s, n, -1).transpose(0, 2, 1, 3)

def split_columns(p):
    out = []
    start = 0
    for w in IN_SPLITS:
        out.append(p[..., start:start + w])
        start += w
    return out

def to_query_blocks(t):
    b, h, s, d = t.shape
    return t.reshape(b, h, s // Q_BLOCK, Q_BLOCK, d).transpose(2, 0, 1, 3, 4)

def from_query_blocks(o):
    nb, b, h, qb, d = o.shape
    return o.transpose(1, 2, 0, 3, 4).reshape(b, h, nb * qb, d)

def stick_breaking_attention(q, k, v):
    b, h, s, dh = q.shape
    nb = s // Q_BLOCK
    scale = dh ** -0.5
    kpos = jnp.arange(s)

    def block(args):
        qblk, i = args
        qpos = i * Q_BLOCK + jnp.arange(Q_BLOCK)
        z = jnp.einsum('bhqd,bhkd->bhqk', qblk, k).astype(jnp.float32) * scale
        mask = kpos[None, :] < qpos[:, None]
        log_beta = jax.nn.log_sigmoid(z)
        log_one_minus = jnp.where(mask, jax.nn.log_sigmoid(-z), 0.0)
        tail = lax.cumsum(log_one_minus, axis=3, reverse=True) - log_one_minus
        w = jnp.where(mask, jnp.exp(log_beta + tail), 0.0)
        return jnp.einsum('bhqk,bhkd->bhqd', w.astype(v.dtype), v)

    out = lax.map(block, (to_query_blocks(q), jnp.arange(nb)))
    return from_query_blocks(out)

def forgetting_attention(q, k, v, log_f):
    b, h, s, dh = q.shape
    nb = s // Q_BLOCK
    scale = dh ** -0.5
    cum_f = jnp.cumsum(log_f, axis=-1)
    cum_f_blocks = cum_f.reshape(b, h, nb, Q_BLOCK).transpose(2, 0, 1, 3)
    kpos = jnp.arange(s)

    def block(args):
        qblk, fq, i = args
        qpos = i * Q_BLOCK + jnp.arange(Q_BLOCK)
        logits = (jnp.einsum('bhqd,bhkd->bhqk', qblk, k).astype(jnp.float32) * scale
                  + fq[..., None] - cum_f[:, :, None, :])
        logits = jnp.where(kpos[None, :] <= qpos[:, None], logits, -jnp.inf)
        p = jax.nn.softmax(logits, axis=-1)
        return jnp.einsum('bhqk,bhkd->bhqd', p.astype(v.dtype), v)

    out = lax.map(block, (to_query_blocks(q), cum_f_blocks, jnp.arange(nb)))
    return from_query_blocks(out)

def gla_chunked(q, k, v, log_a):
    b, h, s, dk = q.shape
    dv = v.shape[-1]
    c = GLA_CHUNK
    n = s // c
    qc = q.astype(jnp.float32).reshape(b, h, n, c, dk) * dk ** -0.5
    kc = k.astype(jnp.float32).reshape(b, h, n, c, dk)
    vc = v.astype(jnp.float32).reshape(b, h, n, c, dv)
    g = jnp.cumsum(log_a.reshape(b, h, n, c, dk), axis=3)
    g_last = g[:, :, :, -1:, :]
    causal = jnp.tril(jnp.ones((c, c), dtype=bool))[:, :, None]
    diff = g[:, :, :, :, None, :] - g[:, :, :, None, :, :]
    decay = jnp.exp(jnp.where(causal, diff, -jnp.inf))
    scores = jnp.einsum('bhntk,bhnsk,bhntsk->bhnts', qc, kc, decay)
    o_intra = jnp.einsum('bhnts,bhnsv->bhntv', scores, vc)
    q_in = qc * jnp.exp(g)
    k_out = kc * jnp.exp(g_last - g)
    a_chunk = jnp.exp(g_last[:, :, :, 0, :])

    def step(state, inp):
        qi, ki, vi, ai = inp
        o = jnp.einsum('bhtk,bhkv->bhtv', qi, state)
        state = ai[..., None] * state + jnp.einsum('bhsk,bhsv->bhkv', ki, vi)
        return state, o

    state0 = jnp.zeros((b, h, dk, dv), jnp.float32)
    xs = (jnp.moveaxis(q_in, 2, 0), jnp.moveaxis(k_out, 2, 0), jnp.moveaxis(vc, 2, 0), jnp.moveaxis(a_chunk, 2, 0))
    _, o_inter = lax.scan(step, state0, xs)
    o = o_intra + jnp.moveaxis(o_inter, 0, 2)
    return o.reshape(b, h, s, dv)

def alibi_slopes(n):
    return 2.0 ** (-8.0 * jnp.arange(1, n + 1, dtype=jnp.float32) / n)

def dilated_branch(q, k, v, dilation, n_steps, slopes):
    b, h, s, dh = q.shape
    r = dilation
    m = s // r
    blk = DIL_BLOCK
    nb = -(-m // blk)
    mp = nb * blk

    def regroup(t):
        return t.reshape(b, h, m, r, dh).transpose(0, 1, 3, 2, 4)

    qs = jnp.pad(regroup(q), ((0, 0), (0, 0), (0, 0), (0, mp - m), (0, 0))).reshape(b, h, r, nb, blk, dh)

    def key_windows(t):
        tp = jnp.pad(regroup(t), ((0, 0), (0, 0), (0, 0), (blk, mp - m), (0, 0))).reshape(b, h, r, nb + 1, blk, dh)
        return jnp.concatenate([tp[:, :, :, :-1], tp[:, :, :, 1:]], axis=4)

    kw = key_windows(k)
    vw = key_windows(v)
    logits = jnp.einsum('bhrnqd,bhrnkd->bhrnqk', qs, kw).astype(jnp.float32) * dh ** -0.5
    qi = jnp.arange(blk)[:, None]
    kj = jnp.arange(2 * blk)[None, :]
    steps = qi + blk - kj
    key_sub = jnp.arange(nb)[:, None, None] * blk + kj[None] - blk
    valid = (steps >= 0) & (steps <= n_steps) & (key_sub >= 0)
    bias = -slopes[:, None, None] * (steps * r).astype(jnp.float32)
    logits = jnp.where(valid, logits + bias[None, :, None, None], -jnp.inf)
    mx = jnp.max(logits, axis=-1)
    p = jnp.exp(logits - mx[..., None])
    den = jnp.sum(p, axis=-1)
    num = jnp.einsum('bhrnqk,bhrnkd->bhrnqd', p, vw.astype(jnp.float32))

    def ungroup(t):
        extra = t.shape[5:]
        t = t.reshape((b, h, r, mp) + extra)[:, :, :, :m]
        return jnp.moveaxis(t, 2, 3).reshape((b, h, s) + extra)

    return ungroup(num), ungroup(den), ungroup(mx)

def dilated_attention(q, k, v, slopes):
    parts = [dilated_branch(q, k, v, r, w // r, slopes) for (w, r) in DIL_PAIRS]
    mx_all = parts[0][2]
    for part in parts[1:]:
        mx_all = jnp.maximum(mx_all, part[2])
    num = 0.0
    den = 0.0
    for (nu, de, mx) in parts:
        wgt = jnp.exp(mx - mx_all)
        num = num + wgt[..., None] * nu
        den = den + wgt * de
    return num / den[..., None]

def peer_ffn(h, w_query, sub_keys, expert_u, expert_v):
    b, s, d = h.shape
    half = PEER_QUERY_DIM // 2
    tb = PEER_TOKEN_BLOCK
    tokens = h.reshape(-1, tb, d)

    def block(xb):
        qry = jnp.einsum('td,dq->tq', xb, w_query).reshape(tb, PEER_HEADS, 2, half)
        scores = jnp.einsum('thcd,hcnd->thcn', qry, sub_keys).astype(jnp.float32)
        s_top, i_top = lax.top_k(scores, PEER_TOPK)
        cand = s_top[:, :, 0, :, None] + s_top[:, :, 1, None, :]
        cidx = i_top[:, :, 0, :, None] * PEER_N_KEYS + i_top[:, :, 1, None, :]
        best, pos = lax.top_k(cand.reshape(tb, PEER_HEADS, PEER_TOPK * PEER_TOPK), PEER_TOPK)
        eidx = jnp.take_along_axis(cidx.reshape(tb, PEER_HEADS, PEER_TOPK * PEER_TOPK), pos, axis=-1)
        gate = jax.nn.softmax(best, axis=-1)
        u = expert_u[eidx]
        v = expert_v[eidx]
        act = jax.nn.gelu(jnp.einsum('td,thkd->thk', xb, u).astype(jnp.float32), approximate=False)
        return jnp.einsum('thk,thkd->td', (gate * act).astype(v.dtype), v)

    out = lax.map(block, tokens)
    return out.reshape(b, s, d)

def setup_inputs(seed: int = 0) -> dict:
    key = jax.random.key(seed)
    ks = jax.random.split(key, 14)
    f32 = jnp.float32
    x = jax.random.normal(ks[0], (BATCH, SEQ, D_MODEL), f32)
    norm_mix_g = 1.0 + 0.02 * jax.random.normal(ks[1], (DEPTH, D_MODEL), f32)
    w_in = jax.random.normal(ks[2], (DEPTH, D_MODEL, PROJ_W), f32) * D_MODEL ** -0.5
    w_gla_up = jax.random.normal(ks[3], (DEPTH, GLA_GATE_RANK, GLA_QK_W), f32) * GLA_GATE_RANK ** -0.5
    b_gla = 0.1 * jax.random.normal(ks[4], (DEPTH, GLA_QK_W), f32)
    b_fox = 3.0 + 0.1 * jax.random.normal(ks[5], (DEPTH, N_FOX_HEADS), f32)
    head_norm_g = 1.0 + 0.02 * jax.random.normal(ks[6], (DEPTH, N_MIX_HEADS, HEAD_DIM), f32)
    w_out = jax.random.normal(ks[7], (DEPTH, N_MIX_HEADS * HEAD_DIM, D_MODEL), f32) * (N_MIX_HEADS * HEAD_DIM) ** -0.5
    norm_ffn_g = 1.0 + 0.02 * jax.random.normal(ks[8], (DEPTH, D_MODEL), f32)
    w_peer_q = jax.random.normal(ks[9], (DEPTH, D_MODEL, PEER_HEADS * PEER_QUERY_DIM), f32) * D_MODEL ** -0.5
    peer_sub_keys = jax.random.normal(ks[10], (DEPTH, PEER_HEADS, 2, PEER_N_KEYS, PEER_QUERY_DIM // 2), f32) * (PEER_QUERY_DIM // 2) ** -0.5
    peer_u = jax.random.normal(ks[11], (DEPTH, PEER_N_EXPERTS, D_MODEL), f32) * D_MODEL ** -0.5
    peer_v = 0.25 * jax.random.normal(ks[12], (DEPTH, PEER_N_EXPERTS, D_MODEL), f32)
    norm_final_g = 1.0 + 0.02 * jax.random.normal(ks[13], (D_MODEL,), f32)
    return {'x': x, 'norm_mix_g': norm_mix_g, 'w_in': w_in, 'w_gla_up': w_gla_up, 'b_gla': b_gla,
            'b_fox': b_fox, 'head_norm_g': head_norm_g, 'w_out': w_out, 'norm_ffn_g': norm_ffn_g,
            'w_peer_q': w_peer_q, 'peer_sub_keys': peer_sub_keys, 'peer_u': peer_u, 'peer_v': peer_v,
            'norm_final_g': norm_final_g}

def reference(x, norm_mix_g, w_in, w_gla_up, b_gla, b_fox, head_norm_g, w_out, norm_ffn_g,
              w_peer_q, peer_sub_keys, peer_u, peer_v, norm_final_g):
    b, s, _ = x.shape
    slopes = alibi_slopes(N_DIL_HEADS)
    h0 = N_SB_HEADS
    h1 = h0 + N_GLA_HEADS
    h2 = h1 + N_DIL_HEADS
    for l in range(DEPTH):
        hn = rms_norm(x, norm_mix_g[l])
        proj = jnp.einsum('bsd,dp->bsp', hn, w_in[l])
        (sb_q, sb_k, sb_v, gla_q, gla_k, gla_v, gla_r, gla_gd,
         dil_q, dil_k, dil_v, fox_q, fox_k, fox_v, fox_f) = split_columns(proj)
        g = head_norm_g[l]

        o_sb = stick_breaking_attention(to_heads(sb_q, N_SB_HEADS), to_heads(sb_k, N_SB_HEADS),
                                        to_heads(sb_v, N_SB_HEADS))
        o_sb = head_rms_norm(o_sb, g[:h0])

        gate_logit = (jnp.einsum('bsr,rk->bsk', gla_gd, w_gla_up[l]) + b_gla[l]).astype(jnp.float32)
        log_a = jax.nn.log_sigmoid(gate_logit) / GLA_GATE_TAU
        o_gla = gla_chunked(to_heads(gla_q, N_GLA_HEADS), to_heads(gla_k, N_GLA_HEADS),
                            to_heads(gla_v, N_GLA_HEADS), to_heads(log_a, N_GLA_HEADS))
        o_gla = head_rms_norm(o_gla, g[h0:h1]) * jax.nn.silu(to_heads(gla_r, N_GLA_HEADS).astype(jnp.float32))

        o_dil = dilated_attention(to_heads(dil_q, N_DIL_HEADS), to_heads(dil_k, N_DIL_HEADS),
                                  to_heads(dil_v, N_DIL_HEADS), slopes)
        o_dil = head_rms_norm(o_dil, g[h1:h2])

        log_f = jax.nn.log_sigmoid(fox_f.astype(jnp.float32) + b_fox[l].astype(jnp.float32))
        o_fox = forgetting_attention(to_heads(fox_q, N_FOX_HEADS), to_heads(fox_k, N_FOX_HEADS),
                                     to_heads(fox_v, N_FOX_HEADS), log_f.transpose(0, 2, 1))
        o_fox = head_rms_norm(o_fox, g[h2:])

        o = jnp.concatenate([o_sb, o_gla, o_dil, o_fox], axis=1)
        o = o.transpose(0, 2, 1, 3).reshape(b, s, N_MIX_HEADS * HEAD_DIM).astype(x.dtype)
        x = x + jnp.einsum('bsm,md->bsd', o, w_out[l])
        x = x + peer_ffn(rms_norm(x, norm_ffn_g[l]), w_peer_q[l], peer_sub_keys[l], peer_u[l], peer_v[l])
    return rms_norm(x, norm_final_g)


_drawn_inputs = setup_inputs


def setup_inputs(seed=0):
    import zlib

    import numpy as np

    out = dict(_drawn_inputs(seed))
    spreads = {}
    factors = {'b_gla': 3.005, 'norm_ffn_g': 2.881, 'norm_final_g': 2.754}
    for name, (base, spread) in spreads.items():
        noise = np.random.default_rng([zlib.crc32(name.encode()), seed]).standard_normal(out[name].shape)
        drawn = base * np.exp(spread * noise) if base else spread * noise
        out[name] = jnp.asarray(drawn.astype(out[name].dtype))
    for name, factor in factors.items():
        out[name] = (out[name] * factor).astype(out[name].dtype)
    return out
```

```python
from contextlib import ExitStack

import numpy as np

import concourse.bass as bass
from concourse import mybir

ALU = mybir.AluOpType
ACT = mybir.ActivationFunctionType
AX = mybir.AxisListType
F32 = mybir.dt.float32
U32 = mybir.dt.uint32

P = 128
T = 256
NTB = T // P
D = 1024
KT = D // P
DEPTH = 2
EPS = 1e-6
HD = 64
HV = HD + 1
NH = 16
GH = 4
DK = 32
CH = 32
NCH = T // CH
TAU = 16.0
RANK = 16
FOX0 = 32
SMALL = FOX0 + GH
HEADS = 8
TOPK = 16
NK = 128
HK = HEADS * TOPK
NEG = -1e30
LOWEST = -3.0e38

SLOTS = 4
UF = 2048
U_IN, U_OUT, U_PQ = 12, 4, 8
U_DENSE = U_IN + U_OUT + U_PQ
PAIRS = NK // 2
UNITS = U_DENSE + 2 * PAIRS
assert UNITS % SLOTS == 0

SIDE = {}
_at = 0
for _name, _n in (("subk", 2 * HEADS * NK), ("small", KT * SMALL), ("up", P), ("b_gla", 1), ("b_fox", 1),
                  ("g_mix", KT), ("g_head", KT), ("g_ffn", KT)):
    SIDE[_name] = (_at, _at + _n)
    _at += _n
SIDE_F = _at

MC = {}
_at = 0
for _name, _n in (("tri", P), ("ones", T), ("k_lt_q", P), ("k_le_q", P), ("dil_count", 3 * P),
                  ("dil_bias", GH * 3 * P), ("fox_mask", 3 * P), ("head_sel", GH * P)):
    MC[_name] = (_at, _at + _n)
    _at += _n
MC_F = _at

KQ = 3 * P
CHOFF = [sum(CH * (c + 1) for c in range(n)) for n in range(NCH + 1)]

GROUPS = T // 4


def host_constants():
    p = np.arange(P)[:, None]
    f = np.arange(P)[None, :]
    mc = np.zeros((P, MC_F), np.float32)

    def put(name, a):
        s, e = MC[name]
        mc[:a.shape[0], s:e] = a.reshape(a.shape[0], -1)

    put("tri", (p > f).astype(np.float32))
    put("ones", np.ones((P, T), np.float32))
    put("k_lt_q", (p < f).astype(np.float32))
    put("k_le_q", (p <= f).astype(np.float32))
    d = np.stack([p - f, p - f + P, p - f], 1)
    ok = d >= 0
    count = ok * ((d <= 128).astype(int) + (d % 4 == 0) + (d % 16 == 0))
    put("dil_count", count.astype(np.float32))
    slopes = 2.0 ** (-8.0 * np.arange(1, GH + 1) / GH)
    bias = np.where(count[:, None] > 0, -slopes[None, :, None, None] * d[:, None], NEG)
    put("dil_bias", bias.astype(np.float32))
    put("fox_mask", np.where(ok, 0.0, NEG).astype(np.float32))
    sel = np.zeros((P, GH, P), np.float32)
    for h in range(GH):
        sel[FOX0 + h, h] = 1.0
    put("head_sel", sel)
    fixed = np.concatenate([np.eye(P, dtype=np.float32), np.broadcast_to(f, (P, P)).astype(np.float32)], 1)
    return mc, np.ascontiguousarray(fixed)


def build(nc, x_in, stream, side_in, mixc_in, fixed_in, gfin_in, out):
    with ExitStack() as ctx:
        def sb(name, cols, dt=F32):
            return ctx.enter_context(nc.sbuf_tensor(name, [P, cols], dt))

        def sem(name):
            return ctx.enter_context(nc.semaphore(name))

        X = sb("X", NTB * D)[:].rearrange("p (b d) -> p b d", b=NTB)
        HT = sb("HT", KT * T)[:].rearrange("p (k t) -> p k t", k=KT)
        REG = sb("REG", NK * T)
        RING = sb("RING", SLOTS * UF)
        SIDEB = sb("SIDEB", SIDE_F)
        FIX = sb("FIX", 2 * P)
        ROUTE = sb("ROUTE", 3 * T)[:].rearrange("p (a t) -> p a t", a=3)
        WORK = sb("WORK", 2048)
        TINY = sb("TINY", 512)
        psum = ctx.enter_context(nc.psum_tensor("psum", [P, 8, 512], F32))

        ident = FIX[:, 0:P]
        iota = FIX[:, P:2 * P]

        def side(name):
            s, e = SIDE[name]
            return SIDEB[:, s:e]

        subk = side("subk").rearrange("p (c n) -> p c n", n=NK)
        wsmall = side("small").rearrange("p (k c) -> p k c", k=KT)

        at = [0]

        def reg(n):
            at[0] += n
            assert at[0] <= NK * T
            return REG[:, at[0] - n:at[0]]

        mixc = reg(MC_F)

        def mc(name):
            s, e = MC[name]
            return mixc[:, s:e]

        XN = reg(NTB * D).rearrange("p (b d) -> p b d", b=NTB)
        JUNK = reg(D)
        QK = reg(14 * T).rearrange("p (c t) -> p c t", t=T)
        AQ, AK, BQ, BK, CQ, CK, DQ, DKEY = 0, 2, 4, 5, 6, 8, 10, 12
        VN = reg(NTB * NH * HV).rearrange("p (b h v) -> p b h v", b=NTB, h=NH)
        RN = reg(NTB * T).rearrange("p (b c) -> p b c", b=NTB)
        SIG = reg(NTB * T).rearrange("p (b c) -> p b c", b=NTB)
        GDT = reg(T)
        GLY, GLA_A, GLC, GLQ = reg(T), reg(T), reg(T), reg(T)
        FOXY, FOXA, FOXC = reg(T), reg(T), reg(T)
        KDEC = reg(CHOFF[NCH])
        PT = [reg(GH * KQ).rearrange("p (h c) -> p h c", h=GH) for _ in range(4)]
        scores_at = at[0]
        SA, SB_, SC, SD = [reg(GH * KQ).rearrange("p (h c) -> p h c", h=GH) for _ in range(4)]
        OALL = reg(NTB * NH * HV).rearrange("p (b h v) -> p b h v", b=NTB, h=NH)
        OSQ = REG[:, scores_at:scores_at + NTB * D].rearrange("p (b h v) -> p b h v", b=NTB, h=NH)
        OT = REG[:, scores_at + 2 * GH * KQ:scores_at + 2 * GH * KQ + KT * T].rearrange("p (k t) -> p k t", k=KT)
        ONRM = XN

        at[0] = MC_F + NTB * D + D
        QRY = reg(2 * HEADS * T).rearrange("p (c t) -> p c t", t=T)
        SCO = reg(2 * HEADS * NK).rearrange("p (c n) -> p c n", n=NK)
        SCO2 = reg(2 * HEADS * NK).rearrange("p (c n) -> p c n", n=NK)
        CAND = reg(HEADS * 256).rearrange("p (h n) -> p h n", h=HEADS)
        CAND2 = reg(HEADS * 256).rearrange("p (h n) -> p h n", h=HEADS)
        PICK = reg(HEADS * 256).rearrange("p (h k a) -> p h k a", h=HEADS, k=TOPK)
        PICK2 = reg(HEADS * 256).rearrange("p (h k a) -> p h k a", h=HEADS, k=TOPK)
        TOPV = reg(2 * HK).rearrange("p (c k) -> p c k", k=TOPK)
        TOPI = reg(2 * HK).bitcast(U32).rearrange("p (c k) -> p c k", k=TOPK)
        TOPF = reg(2 * HK).rearrange("p (h c k) -> p h c k", c=2, k=TOPK)
        BEST = reg(HK).rearrange("p (h k) -> p h k", k=TOPK)
        POS = reg(HK).bitcast(U32).rearrange("p (h k) -> p h k", k=TOPK)
        POSA = reg(2 * HK).bitcast(U32).rearrange("p (c h k) -> p c h k", c=2, k=TOPK)
        POSF = reg(2 * HK).rearrange("p (c h k) -> p c h k", c=2, k=TOPK)
        CHOSEN = reg(3 * HK).rearrange("p (a c) -> p a c", a=3)
        GSH = reg(HK).rearrange("p (h k) -> p h k", k=TOPK)
        G = REG[:, :].rearrange("p (t j) -> p t j", j=NK)

        OH = WORK[:, :].rearrange("p (b a t n) -> p b a t n", b=2, a=2, t=4)
        GEL = WORK[:, 0:2 * T].rearrange("p (b t) -> p b t", b=2)
        WT = WORK[:, 2 * T:4 * T].rearrange("p (b t) -> p b t", b=2)

        SUMSQ, VAR, RS0, RT1 = TINY[:, 0:2], TINY[:, 2:4], TINY[:, 4:6], TINY[:, 6:8]
        RSTD = TINY[:, 8:10]
        RMID, NRMID = TINY[:, 16:16 + NCH], TINY[:, 24:24 + NCH]
        MAXN = TINY[:, 32:48].rearrange("p (g b h) -> p g b h", g=2, b=NTB)
        RDEN = TINY[:, 48:64].rearrange("p (b h) -> p b h", b=NTB)
        HSS, HVAR, HR0, HR1, HRS = [TINY[:, 64 + 32 * n:96 + 32 * n] for n in range(5)]
        GSUM, GREC = TINY[:, 256:264], TINY[:, 264:272]

        unit_loaded = [sem(f"unit_loaded{n}") for n in range(SLOTS)]
        unit_used = sem("unit_used")
        start_loaded = sem("start_loaded")
        side_loaded = sem("side_loaded")
        mixc_loaded = sem("mixc_loaded")
        gfin_loaded = sem("gfin_loaded")
        sumsq_done = sem("sumsq_done")
        var_ready = sem("var_ready")
        rstd_rough = sem("rstd_rough")
        xn_ready = sem("xn_ready")
        xt_done = sem("xt_done")
        ht_ready = sem("ht_ready")
        small_done = sem("small_done")
        gd_ready = sem("gd_ready")
        gl_done = sem("gl_done")
        gly_ready = sem("gly_ready")
        gls_ready = sem("gls_ready")
        glc_ready = sem("glc_ready")
        gle_ready = sem("gle_ready")
        glq_ready = sem("glq_ready")
        foxy_ready = sem("foxy_ready")
        foxs_ready = sem("foxs_ready")
        foxc_ready = sem("foxc_ready")
        foxb_done = sem("foxb_done")
        foxb_read = sem("foxb_read")
        proj_done = sem("proj_done")
        proj_read = sem("proj_read")
        r_exp = sem("r_exp")
        a_scores = sem("a_scores")
        a_soft = sem("a_soft")
        a_sp = sem("a_sp")
        a_tail = sem("a_tail")
        a_logw = sem("a_logw")
        a_exp = sem("a_exp")
        b_zeroed = sem("b_zeroed")
        b_scores = sem("b_scores")
        b_off = sem("b_off")
        c_scores = sem("c_scores")
        c_logits = sem("c_logits")
        c_exp = sem("c_exp")
        c_prob = sem("c_prob")
        c_flip = sem("c_flip")
        d_scores = sem("d_scores")
        d_logits = sem("d_logits")
        d_exp = sem("d_exp")
        d_flip = sem("d_flip")
        pt_ready = sem("pt_ready")
        pv_done = sem("pv_done")
        o_ready = sem("o_ready")
        o_scaled = sem("o_scaled")
        o_sq = sem("o_sq")
        hvar_ready = sem("hvar_ready")
        hrstd_rough = sem("hrstd_rough")
        onrm_ready = sem("onrm_ready")
        ot_done = sem("ot_done")
        ot_ready = sem("ot_ready")
        mix_done = sem("mix_done")
        x_mixed = sem("x_mixed")
        pq_done = sem("pq_done")
        pq_read = sem("pq_read")
        score_done = sem("score_done")
        score_read = sem("score_read")
        topk_used = sem("topk_used")
        gate_shift = sem("gate_shift")
        gate_exp = sem("gate_exp")
        chosen_ready = sem("chosen_ready")
        route_done = sem("route_done")
        route_ready = sem("route_ready")
        onehot_ready = sem("onehot_ready")
        gate_done = sem("gate_done")
        gate_read = sem("gate_read")
        act_done = sem("act_done")
        gelu_ready = sem("gelu_ready")
        wt_ready = sem("wt_ready")
        wt_used = sem("wt_used")
        dense_done = sem("dense_done")
        x_new = sem("x_new")
        y_ready = sem("y_ready")
        stored = sem("stored")

        block = ctx.enter_context(nc.Block())

        @block.sync
        def _(sp):
            def load(n, slot):
                sp.dma_start(RING[:, slot * UF:(slot + 1) * UF], stream[n]).then_inc(unit_loaded[slot], 16)

            for n in range(SLOTS):
                load(n, n)
            with sp.Fori(1, DEPTH * UNITS // SLOTS) as r:
                for slot in range(SLOTS):
                    sp.wait_ge(unit_used, r * SLOTS + slot - (SLOTS - 1))
                    load(r * SLOTS + slot, slot)
            sp.wait_ge(y_ready, 1)
            sp.dma_start(out.rearrange("a (b p) d -> p (a b) d", p=P), XN).then_inc(stored, 16)
            sp.wait_ge(stored, 16)

        @block.gpsimd
        def _(pool):
            pool.dma_start(X, x_in.rearrange("a (b p) d -> p (a b) d", p=P)).then_inc(start_loaded, 16)
            pool.dma_start(FIX[:, :], fixed_in).then_inc(start_loaded, 16)
            pool.wait_ge(x_new, DEPTH * 4)
            pool.dma_start(JUNK, gfin_in).then_inc(gfin_loaded, 16)

        @block.scalar
        def _(act):
            def rough_rsqrt(dst, tmp, src):
                act.activation(tmp, src, ACT.Ln)
                act.drain()
                return act.activation(dst, tmp, ACT.Exp, scale=-0.5)

            def norm_stats(n):
                for b in range(NTB):
                    last = act.activation(XN[:, b, :], X[:, b, :], ACT.Square, accum_out=SUMSQ[:, b:b + 1])
                last.then_inc(sumsq_done, 1)
                act.wait_ge(var_ready, n + 1)
                rough_rsqrt(RS0, RT1, VAR).then_inc(rstd_rough, 1)

            def softplus_tail(dst, src):
                act.activation(dst, src, ACT.Abs)
                act.drain()
                act.activation(dst, dst, ACT.Exp, scale=-1.0)
                act.drain()
                return act.activation(dst, dst, ACT.Ln, bias=1.0)

            act.wait_ge(start_loaded, 32)
            with act.Fori(0, DEPTH) as l:
                act.wait_ge(x_new, l * 4)
                act.dma_start(SIDEB[:, :], side_in[l]).then_inc(side_loaded, 16)
                act.dma_start(mixc, mixc_in).then_inc(mixc_loaded, 16)
                norm_stats(l * 2)
                act.wait_ge(small_done, l + 1)
                act.copy(GDT[0:RANK, :], psum[0:RANK, 7, 0:T]).then_inc(gd_ready, 1)
                for u in range(U_IN):
                    if u == 2:
                        act.wait_ge(gly_ready, l + 1)
                        softplus_tail(GLA_A, GLY).then_inc(gls_ready, 1)
                        act.wait_ge(foxy_ready, l + 1)
                        softplus_tail(FOXA[FOX0:SMALL, :], FOXY[FOX0:SMALL, :]).then_inc(foxs_ready, 1)
                    act.wait_ge(proj_done, l * U_IN + u + 1)
                    src = psum[:, u % 4, :]
                    if u < 7:
                        act.activation(QK[:, 2 * u:2 * u + 2, :], src.rearrange("p (c t) -> p c t", c=2), ACT.Copy,
                                       scale=0.125 if u in (0, 3, 5) else 1.0).then_inc(proj_read, 1)
                    elif u < 11:
                        if u == 7:
                            act.wait_ge(b_zeroed, l + 1)
                        h = GH * (u - 7)
                        act.activation(VN[:, :, h:h + GH, 0:HD],
                                       src.rearrange("p (b h v) -> p b h v", b=NTB, h=GH), ACT.Copy).then_inc(proj_read, 1)
                    else:
                        act.activation(RN[:, :, :], src.rearrange("p (b c) -> p b c", b=NTB), ACT.Copy).then_inc(proj_read, 1)
                act.drain()
                act.activation(SIG[:, :, :], RN[:, :, :], ACT.Exp, scale=-1.0).then_inc(r_exp, 1)
                act.wait_ge(glc_ready, l + 1)
                for c in range(NCH):
                    act.activation(KDEC[:, CHOFF[c]:CHOFF[c + 1]], GLC[:, 0:CH * (c + 1)], ACT.Exp,
                                   bias=NRMID[:, c:c + 1], scale=1.0 / TAU)
                act.activation(GLQ, GLQ, ACT.Exp, scale=-1.0 / TAU).then_inc(gle_ready, 1)
                act.wait_ge(a_scores, l + 1)
                softplus_tail(SA[:, :, :], psum[:, 0:GH, 0:KQ]).then_inc(a_soft, 1)
                act.wait_ge(c_logits, l + 1)
                for b in range(NTB):
                    for h in range(GH):
                        cols = slice(0, P) if b == 0 else slice(P, KQ)
                        last = act.activation(SC[:, h, cols], SC[:, h, cols], ACT.Exp, bias=MAXN[:, 0, b, h:h + 1])
                last.then_inc(c_exp, 1)
                act.wait_ge(a_logw, l + 1)
                act.activation(PT[0][:, :, :], SA[:, :, :], ACT.Exp).then_inc(a_exp, 1)
                act.wait_ge(c_flip, l + 1)
                act.copy(PT[2][:, :, :], psum[:, GH:2 * GH, 0:KQ]).then_inc(pt_ready, 1)
                act.wait_ge(b_scores, l + 1)
                act.copy(PT[1][:, :, P:2 * P], psum[:, 0:GH, P:2 * P]).then_inc(b_off, 1)
                act.wait_ge(d_logits, l + 1)
                for b in range(NTB):
                    for h in range(GH):
                        cols = slice(0, P) if b == 0 else slice(P, KQ)
                        last = act.activation(SD[:, h, cols], SD[:, h, cols], ACT.Exp, bias=MAXN[:, 1, b, h:h + 1])
                last.then_inc(d_exp, 1)
                act.wait_ge(d_flip, l + 1)
                act.copy(PT[3][:, :, :], psum[:, GH:2 * GH, 0:KQ]).then_inc(pt_ready, 1)
                act.wait_ge(o_scaled, l + 1)
                act.activation(OSQ[:, :, :, :], OALL[:, :, :, 0:HD], ACT.Square).then_inc(o_sq, 1)
                act.wait_ge(hvar_ready, l + 1)
                rough_rsqrt(HR0, HR1, HVAR).then_inc(hrstd_rough, 1)
                for n in range(4):
                    act.wait_ge(mix_done, l * 4 + n + 1)
                    last = act.copy(X[:, n // 2, (n % 2) * 512:(n % 2 + 1) * 512], psum[:, n, :])
                last.then_inc(x_mixed, 1)
                act.drain()
                norm_stats(l * 2 + 1)
                for u in range(U_PQ):
                    act.wait_ge(pq_done, l * U_PQ + u + 1)
                    act.copy(QRY[:, 2 * u:2 * u + 2, :],
                             psum[:, u % 4, :].rearrange("p (c t) -> p c t", c=2)).then_inc(pq_read, 1)
                for b in range(NTB):
                    if b:
                        act.wait_ge(topk_used, l * NTB + b)
                    for n in range(2):
                        act.wait_ge(score_done, l * 2 * NTB + 2 * b + n + 1)
                        act.copy(SCO[:, 8 * n:8 * n + 8, :], psum[:, 4 + 2 * n:6 + 2 * n, :]
                                 .rearrange("p b (c n) -> p (b c) n", n=NK)).then_inc(score_read, 1)
                    act.wait_ge(gate_shift, l * NTB + b + 1)
                    act.activation(GSH[:, :, :], GSH[:, :, :], ACT.Exp).then_inc(gate_exp, 1)
                with act.Fori(0, GROUPS // 2) as g2:
                    for s in range(2):
                        act.wait_ge(gate_done, l * GROUPS + g2 * 2 + s + 1)
                        act.copy(G[:, bass.ds(g2 * 8 + s * 4, 4), :],
                                 psum[:, 6 + s, :].rearrange("p (t j) -> p t j", t=4)).then_inc(gate_read, 1)
                with act.Fori(0, NK // 4) as j4:
                    for s in range(4):
                        act.wait_ge(act_done, l * NK + j4 * 4 + s + 1)
                        act.wait_ge(wt_ready, l * NK + j4 * 4 + s - 1 if s >= 1 else l * NK + j4 * 4)
                        act.activation(GEL[:, s % 2, :], psum[:, 4 + s % 2, 0:T], ACT.Gelu).then_inc(gelu_ready, 1)
                act.wait_ge(dense_done, l + 1)
                for n in range(4):
                    act.copy(X[:, n // 2, (n % 2) * 512:(n % 2 + 1) * 512], psum[:, n, :]).then_inc(x_new, 1)
                act.drain()
            norm_stats(DEPTH * 2)

        @block.vector
        def _(dve):
            def refine_rsqrt(dst, tmp, rough, var):
                dve.tensor_tensor(tmp, rough, rough, ALU.mult)
                dve.drain()
                dve.tensor_tensor(tmp, tmp, var, ALU.mult)
                dve.drain()
                dve.tensor_scalar(tmp, tmp, -0.5, 1.5, ALU.mult, ALU.add)
                dve.drain()
                dve.tensor_tensor(dst, rough, tmp, ALU.mult)
                dve.drain()

            def norm_rstd(n):
                dve.wait_ge(sumsq_done, n + 1)
                dve.tensor_scalar(VAR, SUMSQ, 1.0 / D, EPS, ALU.mult, ALU.add).then_inc(var_ready, 1)
                dve.wait_ge(rstd_rough, n + 1)
                refine_rsqrt(RSTD, RT1, RS0, VAR)

            def norm(n, gain):
                norm_rstd(n)
                for b in range(NTB):
                    dve.tensor_scalar(XN[:, b, :], X[:, b, :], RSTD[:, b:b + 1], None, ALU.mult).then_inc(xn_ready, 1)
                for m in range(4):
                    dve.wait_ge(xt_done, n * 4 + m + 1)
                    half = m % 2
                    dve.tensor_tensor(HT[:, 4 * half:4 * half + 4, (m // 2) * P:(m // 2 + 1) * P],
                                      psum[:, m, :].rearrange("p (k t) -> p k t", k=4),
                                      gain[:, 4 * half:4 * half + 4].unsqueeze(2).to_broadcast([P, 4, P]),
                                      ALU.mult).then_inc(ht_ready, 1)

            def diagonal(t):
                return t.rearrange("p h (b q) -> p h b q", b=3)[:, :, 0:3:2, :]

            def masked(t, src, name):
                m = mc(name).unsqueeze(1).to_broadcast([P, 2, P]).unsqueeze(1).to_broadcast([P, GH, 2, P])
                return dve.tensor_tensor(diagonal(t), diagonal(src), m, ALU.mult)

            def row_max(src, g):
                dve.tensor_reduce(MAXN[:, g, 0, :], src[:, :, 0:P], AX.X, ALU.max)
                dve.tensor_reduce(MAXN[:, g, 1, :], src[:, :, P:KQ], AX.X, ALU.max)
                dve.drain()
                return dve.tensor_scalar(MAXN[:, g, :, :], MAXN[:, g, :, :], -1.0, None, ALU.mult)

            def take_o(l, g, bank, order):
                dve.wait_ge(pv_done, l * 4 + order)
                for b in range(NTB):
                    last = dve.tensor_copy(OALL[:, b, GH * g:GH * g + GH, :],
                                           psum[:, bank + b, 0:GH * HV].rearrange("p (h v) -> p h v", h=GH))
                last.then_inc(o_ready, 1)

            dve.wait_ge(start_loaded, 32)
            with dve.Fori(0, DEPTH) as l:
                dve.wait_ge(x_new, l * 4)
                dve.memset(PT[1][:, :, :], 0.0)
                dve.memset(VN[:, :, :, HD:HV], 1.0).then_inc(b_zeroed, 1)
                dve.wait_ge(side_loaded, l * 16 + 16)
                dve.wait_ge(mixc_loaded, l * 16 + 16)
                norm(l * 2, side("g_mix"))
                dve.wait_ge(small_done, l + 1)
                dve.tensor_scalar(FOXY[FOX0:SMALL, :], psum[FOX0:SMALL, 7, 0:T],
                                  side("b_fox")[FOX0:SMALL, :], -1.0, ALU.add, ALU.mult).then_inc(foxy_ready, 1)
                dve.wait_ge(gl_done, l + 1)
                dve.tensor_scalar(GLY, psum[:, 6, 0:T], side("b_gla"), -1.0, ALU.add, ALU.mult).then_inc(gly_ready, 1)
                dve.wait_ge(gls_ready, l + 1)
                dve.scalar_tensor_tensor(GLA_A, GLY, 0.0, GLA_A, ALU.max, ALU.add)
                dve.drain()
                dve.tensor_tensor_scan(GLC, mc("ones"), GLA_A, 0.0, ALU.mult, ALU.add)
                dve.drain()
                mid = GLC.rearrange("p (c s) -> p c s", s=CH)[:, :, CH // 2 - 1:CH // 2]
                dve.tensor_scalar(NRMID.unsqueeze(2), mid, -1.0 / TAU, None, ALU.mult)
                dve.tensor_tensor(GLQ.rearrange("p (c s) -> p c s", s=CH), GLC.rearrange("p (c s) -> p c s", s=CH),
                                  mid.to_broadcast([P, NCH, CH]), ALU.subtract).then_inc(glc_ready, 1)
                dve.wait_ge(foxs_ready, l + 1)
                rows = slice(FOX0, SMALL)
                dve.scalar_tensor_tensor(FOXA[rows, :], FOXY[rows, :], 0.0, FOXA[rows, :], ALU.max, ALU.add)
                dve.drain()
                dve.tensor_tensor_scan(FOXC[rows, :], mc("ones")[rows, :], FOXA[rows, :], 0.0,
                                       ALU.mult, ALU.add).then_inc(foxc_ready, 1)
                dve.wait_ge(r_exp, l + 1)
                dve.tensor_scalar(SIG[:, :, :], SIG[:, :, :], 1.0, None, ALU.add)
                dve.drain()
                dve.reciprocal(SIG[:, :, :], SIG[:, :, :])
                dve.drain()
                dve.tensor_tensor(SIG[:, :, :], SIG[:, :, :], RN[:, :, :], ALU.mult)
                dve.wait_ge(gle_ready, l + 1)
                dve.wait_ge(proj_read, l * U_IN + 3)
                dve.scalar_tensor_tensor(GLQ, GLQ, DK ** -0.5, QK[:, BQ, :], ALU.mult, ALU.mult)
                for c in range(NCH):
                    last = dve.tensor_tensor(KDEC[:, CHOFF[c]:CHOFF[c + 1]], KDEC[:, CHOFF[c]:CHOFF[c + 1]],
                                             QK[:, BK, 0:CH * (c + 1)], ALU.mult)
                last.then_inc(glq_ready, 1)
                dve.wait_ge(foxb_done, l + 1)
                for h in range(GH):
                    fb = psum[:, 4 + h, :]
                    dve.tensor_tensor(SD[:, h, 0:P], fb[:, 0:P], mc("fox_mask")[:, 0:P], ALU.add)
                    last = dve.tensor_tensor(SD[:, h, P:KQ], fb[:, 0:T], mc("fox_mask")[:, P:KQ], ALU.add)
                last.then_inc(foxb_read, 1)
                dve.wait_ge(c_scores, l + 1)
                dve.tensor_tensor(SC[:, :, :], psum[:, GH:2 * GH, 0:KQ],
                                  mc("dil_bias").rearrange("p (h c) -> p h c", h=GH), ALU.add)
                dve.drain()
                row_max(SC, 0).then_inc(c_logits, 1)
                dve.wait_ge(a_soft, l + 1)
                dve.scalar_tensor_tensor(SA[:, :, :], psum[:, 0:GH, 0:KQ], 0.0, SA[:, :, :], ALU.max, ALU.add)
                dve.drain()
                dve.tensor_tensor(SB_[:, :, :], psum[:, 0:GH, 0:KQ], SA[:, :, :], ALU.subtract)
                dve.drain()
                masked(SA, SA, "k_lt_q").then_inc(a_sp, 1)
                dve.wait_ge(c_exp, l + 1)
                dve.tensor_tensor(SC[:, :, :], SC[:, :, :],
                                  mc("dil_count").unsqueeze(1).to_broadcast([P, GH, KQ]), ALU.mult).then_inc(c_prob, 1)
                dve.wait_ge(a_tail, l + 1)
                dve.tensor_tensor(SA[:, :, :], SB_[:, :, :], psum[:, 0:GH, 0:KQ], ALU.subtract).then_inc(a_logw, 1)
                dve.wait_ge(a_exp, l + 1)
                masked(PT[0], PT[0], "k_lt_q").then_inc(pt_ready, 1)
                take_o(l, 0, 0, 1)
                take_o(l, 2, 4, 2)
                dve.wait_ge(b_off, l + 1)
                for m in range(4):
                    r = CH * (m + 1)
                    cols = slice(CH * m, CH * m + CH)
                    mask = mc("k_le_q")[0:r, cols].unsqueeze(1).to_broadcast([r, 2, CH]).unsqueeze(1)\
                        .to_broadcast([r, GH, 2, CH])
                    last = dve.tensor_tensor(diagonal(PT[1])[0:r, :, :, cols],
                                             diagonal(psum[:, 0:GH, 0:KQ])[0:r, :, :, cols], mask, ALU.mult)
                last.then_inc(pt_ready, 1)
                dve.wait_ge(d_scores, l + 1)
                dve.tensor_tensor(SD[:, :, :], psum[:, GH:2 * GH, 0:KQ], SD[:, :, :], ALU.add)
                dve.drain()
                row_max(SD, 1).then_inc(d_logits, 1)
                take_o(l, 1, 0, 3)
                take_o(l, 3, 4, 4)
                dve.drain()
                dve.reciprocal(RDEN, OALL[:, :, 2 * GH:, HD])
                dve.drain()
                dve.tensor_tensor(OALL[:, :, 2 * GH:, 0:HD], OALL[:, :, 2 * GH:, 0:HD],
                                  RDEN.unsqueeze(3).to_broadcast([P, NTB, 2 * GH, HD]), ALU.mult).then_inc(o_scaled, 1)
                dve.wait_ge(o_sq, l + 1)
                dve.tensor_reduce(HSS.rearrange("p (b h) -> p b h", b=NTB), OSQ[:, :, :, :], AX.X, ALU.add)
                dve.drain()
                dve.tensor_scalar(HVAR, HSS, 1.0 / HD, EPS, ALU.mult, ALU.add).then_inc(hvar_ready, 1)
                dve.wait_ge(hrstd_rough, l + 1)
                refine_rsqrt(HRS, HR1, HR0, HVAR)
                onrm = ONRM.rearrange("p b (h v) -> p b h v", h=NH)
                dve.tensor_tensor(onrm, OALL[:, :, :, 0:HD], HRS.rearrange("p (b h) -> p b h", b=NTB).unsqueeze(3)
                                  .to_broadcast([P, NTB, NH, HD]), ALU.mult)
                dve.drain()
                dve.tensor_tensor(ONRM[:, :, T:2 * T], ONRM[:, :, T:2 * T], SIG[:, :, :], ALU.mult).then_inc(onrm_ready, 1)
                for m in range(4):
                    dve.wait_ge(ot_done, l * 4 + m + 1)
                    half = m % 2
                    dve.tensor_tensor(OT[:, 4 * half:4 * half + 4, (m // 2) * P:(m // 2 + 1) * P],
                                      psum[:, m, :].rearrange("p (k t) -> p k t", k=4),
                                      side("g_head")[:, 4 * half:4 * half + 4].unsqueeze(2).to_broadcast([P, 4, P]),
                                      ALU.mult).then_inc(ot_ready, 1)
                norm(l * 2 + 1, side("g_ffn"))
                for b in range(NTB):
                    dve.wait_ge(score_read, l * 2 * NTB + 2 * b + 2)
                    dve.memset(GSUM, 0.0)
                    for c in range(2 * HEADS):
                        dve.max(TOPV[:, c, 0:8], SCO[:, c, :])
                    dve.drain()
                    for c in range(2 * HEADS):
                        dve.max_index(TOPI[:, c, 0:8], TOPV[:, c, 0:8], SCO[:, c, :])
                        last = dve.match_replace(SCO2[:, c, :], TOPV[:, c, 0:8], SCO[:, c, :], LOWEST)
                    last.then_inc(topk_used, 1)
                    dve.drain()
                    for c in range(2 * HEADS):
                        dve.max(TOPV[:, c, 8:16], SCO2[:, c, :])
                    dve.drain()
                    for c in range(2 * HEADS):
                        dve.max_index(TOPI[:, c, 8:16], TOPV[:, c, 8:16], SCO2[:, c, :])
                    v = TOPV.rearrange("p (h c) k -> p h c k", c=2)
                    dve.tensor_tensor(CAND.rearrange("p h (a b) -> p h a b", a=TOPK),
                                      v[:, :, 0, :].unsqueeze(3).to_broadcast([P, HEADS, TOPK, TOPK]),
                                      v[:, :, 1, :].unsqueeze(2).to_broadcast([P, HEADS, TOPK, TOPK]), ALU.add)
                    dve.drain()
                    dve.tensor_copy(TOPF, TOPI.rearrange("p (h c) k -> p h c k", c=2))
                    for h in range(HEADS):
                        dve.max(BEST[:, h, 0:8], CAND[:, h, :])
                    dve.drain()
                    for h in range(HEADS):
                        dve.max_index(POS[:, h, 0:8], BEST[:, h, 0:8], CAND[:, h, :])
                        dve.match_replace(CAND2[:, h, :], BEST[:, h, 0:8], CAND[:, h, :], LOWEST)
                    dve.drain()
                    for h in range(HEADS):
                        dve.max(BEST[:, h, 8:16], CAND2[:, h, :])
                    dve.drain()
                    for h in range(HEADS):
                        dve.max_index(POS[:, h, 8:16], BEST[:, h, 8:16], CAND2[:, h, :])
                    dve.tensor_tensor(GSH, BEST, BEST[:, :, 0:1].to_broadcast([P, HEADS, TOPK]),
                                      ALU.subtract).then_inc(gate_shift, 1)
                    dve.drain()
                    dve.tensor_scalar(POSA[:, 0], POS, 4, None, ALU.logical_shift_right)
                    dve.tensor_scalar(POSA[:, 1], POS, TOPK - 1, None, ALU.bitwise_and)
                    dve.drain()
                    dve.tensor_copy(POSF, POSA)
                    dve.drain()
                    if b:
                        dve.wait_ge(route_done, l * NTB + b)
                    small_iota = iota[:, 0:TOPK].unsqueeze(1).to_broadcast([P, TOPK, TOPK]).unsqueeze(1)\
                        .to_broadcast([P, HEADS, TOPK, TOPK])
                    for c, pick in ((0, PICK), (1, PICK2)):
                        dve.tensor_tensor(pick, POSF[:, c].unsqueeze(3).to_broadcast([P, HEADS, TOPK, TOPK]),
                                          small_iota, ALU.is_equal)
                    dve.drain()
                    for c, pick in ((0, PICK), (1, PICK2)):
                        dve.tensor_tensor(pick, pick, TOPF[:, :, c, :].unsqueeze(2)
                                          .to_broadcast([P, HEADS, TOPK, TOPK]), ALU.mult)
                    dve.drain()
                    for c, pick in ((0, PICK), (1, PICK2)):
                        dve.tensor_reduce(CHOSEN[:, c, :].rearrange("p (h k) -> p h k", h=HEADS), pick, AX.X, ALU.add)
                    dve.wait_ge(gate_exp, l * NTB + b + 1)
                    dve.tensor_reduce(GSUM, GSH, AX.X, ALU.add)
                    dve.drain()
                    dve.reciprocal(GREC, GSUM)
                    dve.drain()
                    dve.tensor_tensor(CHOSEN[:, 2, :].rearrange("p (h k) -> p h k", h=HEADS), GSH,
                                      GREC.unsqueeze(2).to_broadcast([P, HEADS, TOPK]), ALU.mult).then_inc(chosen_ready, 1)
                for b in range(NTB):
                    dve.wait_ge(route_done, l * NTB + b + 1)
                    last = dve.tensor_copy(ROUTE[:, :, b * P:(b + 1) * P],
                                           psum[:, 6 + b, 0:3 * P].rearrange("p (a t) -> p a t", a=3))
                last.then_inc(route_ready, 1)
                dve.drain()
                with dve.Fori(0, GROUPS // 2) as g2:
                    for s in range(2):
                        dve.wait_ge(gate_done, l * GROUPS + g2 * 2 + s - 1 if s else l * GROUPS + g2 * 2)
                        for t in range(4):
                            tok = bass.ds(g2 * 8 + s * 4 + t, 1)
                            dve.tensor_scalar(OH[:, s, 0, t, :], iota, ROUTE[:, 0, tok], ROUTE[:, 2, tok],
                                              ALU.is_equal, ALU.mult)
                            last = dve.tensor_scalar(OH[:, s, 1, t, :], iota, ROUTE[:, 1, tok], None, ALU.is_equal)
                        last.then_inc(onehot_ready, 1)
                with dve.Fori(0, NK // 4) as j4:
                    for s in range(4):
                        dve.wait_ge(gelu_ready, l * NK + j4 * 4 + s + 1)
                        dve.wait_ge(wt_used, l * NK + j4 * 4 + s - 1 if s else l * NK + j4 * 4)
                        dve.tensor_tensor(WT[:, s % 2, :].unsqueeze(2), GEL[:, s % 2, :].unsqueeze(2),
                                          G[:, :, bass.ds(j4 * 4 + s, 1)], ALU.mult).then_inc(wt_ready, 1)
            norm_rstd(DEPTH * 2)
            dve.wait_ge(gfin_loaded, 16)
            for b in range(NTB):
                last = dve.scalar_tensor_tensor(XN[:, b, :], X[:, b, :], RSTD[:, b:b + 1], JUNK, ALU.mult, ALU.mult)
            last.then_inc(y_ready, 1)

        @block.tensor
        def _(pe):
            def unit(l, n):
                pe.wait_ge(unit_loaded[n % SLOTS], l * (16 * UNITS // SLOTS) + 16 * (n // SLOTS) + 16)
                return RING[:, (n % SLOTS) * UF:(n % SLOTS + 1) * UF]

            def flip_norm(n):
                for m in range(4):
                    if m % 2 == 0:
                        pe.wait_ge(xn_ready, n * 2 + m // 2 + 1)
                    for k in range(4):
                        last = pe.transpose(psum[:, m, k * P:(k + 1) * P],
                                            XN[:, m // 2, (4 * (m % 2) + k) * P:(4 * (m % 2) + k + 1) * P], ident)
                    last.then_inc(xt_done, 1)

            def columns_first(u, w, bank):
                w = w.rearrange("p (k c) -> p k c", k=KT)
                for c in range(2):
                    for k in range(KT):
                        last = pe.matmul(psum[:, bank, c * T:(c + 1) * T], w[:, k, c * P:(c + 1) * P], HT[:, k, :],
                                         start=(k == 0), stop=(k == KT - 1))
                last.then_inc(unit_used, 1)
                return last

            def pv(g, bank):
                for b in range(NTB):
                    for h in range(GH):
                        o = psum[:, bank + b, h * HV:(h + 1) * HV]
                        if b == 0:
                            last = pe.matmul(o, PT[g][:, h, 0:P], VN[:, 0, GH * g + h, :], start=True, stop=True)
                        else:
                            pe.matmul(o, PT[g][:, h, P:2 * P], VN[:, 0, GH * g + h, :], start=True, stop=False)
                            last = pe.matmul(o, PT[g][:, h, 2 * P:KQ], VN[:, 1, GH * g + h, :], start=False, stop=True)
                last.then_inc(pv_done, 1)

            def qk_scores(q, k, bank):
                for h in range(GH):
                    rows = slice(HD * (h % 2), HD * (h % 2) + HD)
                    qT, kT = QK[rows, q + h // 2, :], QK[rows, k + h // 2, :]
                    pe.matmul(psum[:, bank + h, 0:P], qT[:, 0:P], kT[:, 0:P], start=True, stop=True)
                    last = pe.matmul(psum[:, bank + h, P:KQ], qT[:, P:T], kT[:, 0:T], start=True, stop=True)
                return last

            def flip(src, bank):
                for h in range(GH):
                    for n in range(3):
                        last = pe.transpose(psum[:, bank + h, n * P:(n + 1) * P], src[:, h, n * P:(n + 1) * P], ident)
                return last

            pe.wait_ge(start_loaded, 32)
            with pe.Fori(0, DEPTH) as l:
                pe.wait_ge(side_loaded, l * 16 + 16)
                flip_norm(l * 2)
                pe.wait_ge(ht_ready, l * 8 + 4)
                for k in range(KT):
                    last = pe.matmul(psum[0:SMALL, 7, 0:T], wsmall[:, k, :], HT[:, k, :], start=(k == 0), stop=(k == KT - 1))
                last.then_inc(small_done, 1)
                for u in range(U_IN):
                    w = unit(l, u)
                    if u == 1:
                        pe.wait_ge(gd_ready, l + 1)
                        pe.matmul(psum[:, 6, 0:T], side("up")[0:RANK, :], GDT[0:RANK, :], start=True, stop=True).then_inc(gl_done, 1)
                    if u >= 4:
                        pe.wait_ge(proj_read, l * U_IN + u - 3)
                    if u < 7:
                        columns_first(u, w, u % 4)
                    else:
                        w = w.rearrange("p (k c) -> p k c", k=KT)
                        for b in range(NTB):
                            for k in range(KT):
                                last = pe.matmul(psum[:, u % 4, b * T:(b + 1) * T], HT[:, k, b * P:(b + 1) * P],
                                                 w[:, k, :], start=(k == 0), stop=(k == KT - 1))
                        last.then_inc(unit_used, 1)
                    pe.wait_ge(unit_used, l * UNITS + u + 1)
                    pe.sem_inc(proj_done, 1)
                pe.wait_ge(foxc_ready, l + 1)
                pe.wait_ge(gly_ready, l + 1)
                for h in range(GH):
                    last = pe.matmul(psum[:, 4 + h, 0:T], mc("head_sel")[FOX0:SMALL, h * P:(h + 1) * P],
                                     FOXC[FOX0:SMALL, :], start=True, stop=True)
                last.then_inc(foxb_done, 1)
                pe.wait_ge(proj_read, l * U_IN + U_IN)
                for h in range(GH):
                    rows = slice(HD * (h % 2), HD * (h % 2) + HD)
                    qT, kT = QK[rows, AQ + h // 2, :], QK[rows, AK + h // 2, :]
                    pe.matmul(psum[:, h, 0:T], kT[:, 0:P], qT[:, 0:T], start=True, stop=True)
                    last = pe.matmul(psum[:, h, T:KQ], kT[:, P:T], qT[:, P:T], start=True, stop=True)
                last.then_inc(a_scores, 1)
                pe.wait_ge(foxb_read, l + 1)
                qk_scores(CQ, CK, GH).then_inc(c_scores, 1)
                pe.wait_ge(a_sp, l + 1)
                for h in range(GH):
                    pe.matmul(psum[:, h, 0:T], mc("tri"), SA[:, h, 0:T], start=True, stop=False)
                    pe.matmul(psum[:, h, P:T], mc("ones")[:, 0:P], SA[:, h, T:KQ], start=False, stop=True)
                    last = pe.matmul(psum[:, h, T:KQ], mc("tri"), SA[:, h, T:KQ], start=True, stop=True)
                last.then_inc(a_tail, 1)
                pe.wait_ge(c_prob, l + 1)
                flip(SC, GH).then_inc(c_flip, 1)
                pe.wait_ge(pt_ready, l * 4 + 2)
                pv(0, 0)
                pv(2, 4)
                pe.wait_ge(o_ready, l * 4 + 1)
                pe.wait_ge(glq_ready, l + 1)
                for h in range(GH):
                    rows = slice(DK * h, DK * h + DK)
                    for c in reversed(range(NCH)):
                        for kb in range(c // 4 + 1):
                            m = P if kb < c // 4 else CH * (c % 4 + 1)
                            col = CH * c if kb == 0 else T + CH * (c - 4)
                            last = pe.matmul(psum[0:m, h, col:col + CH],
                                             KDEC[rows, CHOFF[c] + kb * P:CHOFF[c] + kb * P + m],
                                             GLQ[rows, CH * c:CH * c + CH], start=True, stop=True)
                last.then_inc(b_scores, 1)
                pe.wait_ge(o_ready, l * 4 + 2)
                qk_scores(DQ, DKEY, GH).then_inc(d_scores, 1)
                pe.wait_ge(pt_ready, l * 4 + 3)
                pe.wait_ge(b_off, l + 1)
                pv(1, 0)
                pe.wait_ge(d_exp, l + 1)
                flip(SD, GH).then_inc(d_flip, 1)
                pe.wait_ge(pt_ready, l * 4 + 4)
                pv(3, 4)
                pe.wait_ge(onrm_ready, l + 1)
                for m in range(4):
                    for k in range(4):
                        last = pe.transpose(psum[:, m, k * P:(k + 1) * P],
                                            ONRM[:, m // 2, (4 * (m % 2) + k) * P:(4 * (m % 2) + k + 1) * P], ident)
                    last.then_inc(ot_done, 1)
                pe.wait_ge(ot_ready, l * 4 + 4)
                for n in range(4):
                    pe.matmul(psum[:, n, :], ident, X[:, n // 2, (n % 2) * 512:(n % 2 + 1) * 512], start=True, stop=False)
                for u in range(U_OUT):
                    w = unit(l, U_IN + u).rearrange("p (k c) -> p k c", k=2)
                    for n in range(4):
                        for k in range(2):
                            last = pe.matmul(psum[:, n, :], OT[:, 2 * u + k, (n // 2) * P:(n // 2 + 1) * P],
                                             w[:, k, (n % 2) * 512:(n % 2 + 1) * 512],
                                             start=False, stop=(u == U_OUT - 1 and k == 1))
                        if u == U_OUT - 1 and n < 3:
                            last.then_inc(mix_done, 1)
                    last.then_inc(unit_used, 1)
                pe.wait_ge(unit_used, l * UNITS + U_IN + U_OUT)
                pe.sem_inc(mix_done, 1)
                pe.wait_ge(x_mixed, l + 1)
                flip_norm(l * 2 + 1)
                pe.wait_ge(ht_ready, l * 8 + 8)
                for u in range(U_PQ):
                    w = unit(l, U_IN + U_OUT + u)
                    if u >= 4:
                        pe.wait_ge(pq_read, l * U_PQ + u - 3)
                    columns_first(u, w, u % 4)
                    pe.wait_ge(unit_used, l * UNITS + U_IN + U_OUT + u + 1)
                    pe.sem_inc(pq_done, 1)
                pe.wait_ge(pq_read, l * U_PQ + U_PQ)
                for b in range(NTB):
                    if b:
                        pe.wait_ge(score_read, l * 2 * NTB + 2 * b)
                    for c in range(2 * HEADS):
                        last = pe.matmul(psum[:, 4 + c // 4, (c % 4) * NK:(c % 4 + 1) * NK],
                                         QRY[:, c, b * P:(b + 1) * P], subk[:, c, :], start=True, stop=True)
                        if c % 8 == 7:
                            last.then_inc(score_done, 1)
                for b in range(NTB):
                    pe.wait_ge(chosen_ready, l * NTB + b + 1)
                    pe.wait_ge(score_read, l * 2 * NTB + 2 * NTB)
                    for a in range(3):
                        last = pe.transpose(psum[:, 6 + b, a * P:(a + 1) * P], CHOSEN[:, a, :], ident)
                    last.then_inc(route_done, 1)
                pe.wait_ge(route_ready, l + 1)
                for n in range(4):
                    pe.matmul(psum[:, n, :], ident, X[:, n // 2, (n % 2) * 512:(n % 2 + 1) * 512], start=True, stop=False)
                with pe.Fori(0, GROUPS // 2) as g2:
                    for s in range(2):
                        pe.wait_ge(onehot_ready, l * GROUPS + g2 * 2 + s + 1)
                        pe.wait_ge(gate_read, l * GROUPS + g2 * 2 + s - 1 if s else l * GROUPS + g2 * 2)
                        for t in range(4):
                            last = pe.matmul(psum[:, 6 + s, t * NK:(t + 1) * NK], OH[:, s, 0, t, :], OH[:, s, 1, t, :],
                                             start=True, stop=True)
                        last.then_inc(gate_done, 1)

                def first_product(slot, jj, a):
                    u = RING[:, slot * UF:(slot + 1) * UF].rearrange("p (j k i) -> p j k i", j=2, k=KT)
                    for k in range(KT):
                        last = pe.matmul(psum[:, 4 + a, 0:T], u[:, jj, k, :], HT[:, k, :],
                                         start=(k == 0), stop=(k == KT - 1))
                    last.then_inc(act_done, 1)
                    return last

                def second_product(slot, jj, a, stop):
                    v = RING[:, slot * UF:(slot + 1) * UF].rearrange("p (j d) -> p j d", j=2)
                    for n in range(4):
                        last = pe.matmul(psum[:, n, :], WT[:, a, (n // 2) * P:(n // 2 + 1) * P],
                                         v[:, jj, (n % 2) * 512:(n % 2 + 1) * 512], start=False, stop=stop)
                    last.then_inc(wt_used, 1)
                    return last

                def four_columns(j4, final):
                    loaded = l * (16 * UNITS // SLOTS) + (U_DENSE // SLOTS + 1) * 16
                    for s in range(4):
                        if s < 3 or not final:
                            nxt = (s + 1) % 4
                            if nxt % 2 == 0:
                                pe.wait_ge(unit_loaded[nxt], loaded + 16 * j4 + (16 if s == 3 else 0))
                            pe.wait_ge(gelu_ready, l * NK + j4 * 4 + s)
                            first_product(2 * (nxt // 2), nxt % 2, nxt % 2)
                            if nxt % 2 == 1:
                                pe.wait_ge(act_done, l * NK + j4 * 4 + s + 2)
                                pe.sem_inc(unit_used, 1)
                        pe.wait_ge(wt_ready, l * NK + j4 * 4 + s + 1)
                        if s % 2 == 0:
                            pe.wait_ge(unit_loaded[s + 1], loaded + 16 * j4)
                        second_product(2 * (s // 2) + 1, s % 2, s % 2, final and s == 3)
                        if s % 2 == 1:
                            pe.wait_ge(wt_used, l * NK + j4 * 4 + s + 1)
                            pe.sem_inc(unit_used, 1)

                pe.wait_ge(unit_loaded[0], l * (16 * UNITS // SLOTS) + (U_DENSE // SLOTS + 1) * 16)
                pe.wait_ge(gate_read, l * GROUPS + GROUPS)
                first_product(0, 0, 0)
                with pe.Fori(0, NK // 4 - 1) as j4:
                    four_columns(j4, False)
                four_columns(NK // 4 - 1, True)
                pe.sem_inc(dense_done, 1)


def kernel(x, norm_mix_g, w_in, w_gla_up, b_gla, b_fox, head_norm_g, w_out, norm_ffn_g,
           w_peer_q, peer_sub_keys, peer_u, peer_v, norm_final_g):
    import concourse.bacc as bacc
    from concourse.bass_utils import run_bass_kernel_spmd

    f32 = np.float32
    w_in, w_out, w_peer_q = np.asarray(w_in), np.asarray(w_out), np.asarray(w_peer_q)
    peer_u, peer_v = np.asarray(peer_u), np.asarray(peer_v)

    def columns(w):
        return w.reshape(KT, P, -1, 256).transpose(2, 1, 0, 3).reshape(-1, P, UF)

    widths = (256, 256, 256, 128, 128, 256, 256, 16, 256, 256, 256, 256, 256, 256, 4)
    ends = np.cumsum(widths)
    part = [slice(e - w, e) for e, w in zip(ends, widths)]
    order = [0, 1, 3, 4, 8, 9, 11, 12, 2, 5, 10, 13, 6]

    stream = np.empty((DEPTH, UNITS, P, UF), f32)
    sides = np.zeros((DEPTH, P, SIDE_F), f32)
    for l in range(DEPTH):
        stream[l, 0:U_IN] = columns(np.concatenate([w_in[l][:, part[n]] for n in order], 1))
        stream[l, U_IN:U_IN + U_OUT] = w_out[l].reshape(U_OUT, 2, P, D).transpose(0, 2, 1, 3).reshape(U_OUT, P, UF)
        stream[l, U_IN + U_OUT:U_DENSE] = columns(w_peer_q[l])
        u = peer_u[l].reshape(P, PAIRS, 2, KT, P).transpose(1, 4, 2, 3, 0)
        stream[l, U_DENSE::2] = u.reshape(PAIRS, P, UF)
        v = peer_v[l].reshape(P, PAIRS, 2, D).transpose(1, 0, 2, 3)
        stream[l, U_DENSE + 1::2] = v.reshape(PAIRS, P, UF)

        def put(name, a):
            s, e = SIDE[name]
            sides[l, :a.shape[0], s:e] = a.reshape(a.shape[0], -1)

        put("subk", np.asarray(peer_sub_keys)[l].transpose(3, 0, 1, 2))
        small = np.zeros((P, KT, SMALL), f32)
        small[:, :, 0:RANK] = w_in[l][:, part[7]].reshape(KT, P, RANK).transpose(1, 0, 2)
        small[:, :, FOX0:] = w_in[l][:, part[14]].reshape(KT, P, GH).transpose(1, 0, 2)
        put("small", small)
        put("up", np.asarray(w_gla_up)[l])
        put("b_gla", np.asarray(b_gla)[l][:, None])
        sides[l, FOX0:SMALL, SIDE["b_fox"][0]] = np.asarray(b_fox)[l]
        put("g_mix", np.asarray(norm_mix_g)[l].reshape(KT, P).T)
        put("g_head", np.asarray(head_norm_g)[l].reshape(KT, P).T)
        put("g_ffn", np.asarray(norm_ffn_g)[l].reshape(KT, P).T)

    mixc, fixed = host_constants()
    arrays = {
        "x_in": np.ascontiguousarray(x),
        "stream": stream.reshape(DEPTH * UNITS, P, UF),
        "side": sides,
        "mixc": mixc,
        "fixed": fixed,
        "gfin": np.ascontiguousarray(np.broadcast_to(np.asarray(norm_final_g), (P, D))),
    }
    nc = bacc.Bacc("TRN2", target_bir_lowering=False, num_devices=1)
    aps = [nc.dram_tensor(n, a.shape, F32, kind="ExternalInput").ap() for n, a in arrays.items()]
    y = nc.dram_tensor("y", (1, T, D), F32, kind="ExternalOutput").ap()
    build(nc, *aps, y)
    r = run_bass_kernel_spmd(nc, [arrays], core_ids=[0])
    return r.results[0]["y"]
```

```python
from contextlib import ExitStack

import numpy as np

import concourse.bass as bass
from concourse import mybir

ALU = mybir.AluOpType
ACT = mybir.ActivationFunctionType
AX = mybir.AxisListType
F32 = mybir.dt.float32
F32R = mybir.dt.float32r
U32 = mybir.dt.uint32

P = 128
T = 256
NTB = T // P
D = 1024
KT = D // P
DEPTH = 2
EPS = 1e-6
HD = 64
HV = HD + 1
NH = 16
GH = 4
DK = 32
CH = 32
NCH = T // CH
TAU = 16.0
RANK = 16
FOX0 = 32
SMALL = FOX0 + GH
HEADS = 8
TOPK = 16
NK = 128
HK = HEADS * TOPK
NEG = -1e30
LOWEST = -3.0e38

SLOTS = 4
CF = 1024
C_IN, C_OUT, C_PQ = 24, 8, 16
IN_T = 14
M_OUT, M_PQ, M_DENSE = C_IN, C_IN + C_OUT, C_IN + C_OUT + C_PQ
EARLY = 28
LATE = NK - EARLY
SPLITS = M_DENSE + EARLY + 2 * LATE
CARDS = SPLITS + EARLY
assert CARDS % SLOTS == 0 and EARLY % SLOTS == 0 and M_DENSE % SLOTS == 0
M_FIRST = M_DENSE + EARLY
M_STEP = M_FIRST + 1
STEP_PAIRS = (LATE - 2) // 2

SIDE = {}
_at = 0
for _name, _n in (("subk", 2 * HEADS * NK), ("small", KT * SMALL), ("up", P), ("b_gla", 1), ("b_fox", 1),
                  ("g_mix", KT), ("g_head", KT), ("g_ffn", KT)):
    SIDE[_name] = (_at, _at + _n)
    _at += _n
SIDE_F = _at

MC = {}
_at = 0
for _name, _n in (("tri", P), ("ones", T), ("k_lt_q", P), ("k_le_q", P), ("dil_count", 3 * P),
                  ("dil_bias", GH * 3 * P), ("fox_mask", 3 * P), ("head_sel", GH * P)):
    MC[_name] = (_at, _at + _n)
    _at += _n
MC_F = _at

KQ = 3 * P
CHOFF = [sum(CH * (c + 1) for c in range(n)) for n in range(NCH + 1)]

GROUPS = T // 4


def host_constants():
    p = np.arange(P)[:, None]
    f = np.arange(P)[None, :]
    mc = np.zeros((P, MC_F), np.float32)

    def put(name, a):
        s, e = MC[name]
        mc[:a.shape[0], s:e] = a.reshape(a.shape[0], -1)

    put("tri", (p > f).astype(np.float32))
    put("ones", np.ones((P, T), np.float32))
    put("k_lt_q", (p < f).astype(np.float32))
    put("k_le_q", (p <= f).astype(np.float32))
    d = np.stack([p - f, p - f + P, p - f], 1)
    ok = d >= 0
    count = ok * ((d <= 128).astype(int) + (d % 4 == 0) + (d % 16 == 0))
    put("dil_count", count.astype(np.float32))
    slopes = 2.0 ** (-8.0 * np.arange(1, GH + 1) / GH)
    bias = np.where(count[:, None] > 0, -slopes[None, :, None, None] * d[:, None], NEG)
    put("dil_bias", bias.astype(np.float32))
    put("fox_mask", np.where(ok, 0.0, NEG).astype(np.float32))
    sel = np.zeros((P, GH, P), np.float32)
    for h in range(GH):
        sel[FOX0 + h, h] = 1.0
    put("head_sel", sel)
    fixed = np.concatenate([np.eye(P, dtype=np.float32), np.broadcast_to(f, (P, P)).astype(np.float32)], 1)
    return mc, np.ascontiguousarray(fixed)


def build(nc, x_in, stream, side_in, mixc_in, fixed_in, gfin_in, out):
    with ExitStack() as ctx:
        def sb(name, cols, dt=F32):
            return ctx.enter_context(nc.sbuf_tensor(name, [P, cols], dt))

        def sem(name):
            return ctx.enter_context(nc.semaphore(name))

        X = sb("X", NTB * D)[:].rearrange("p (b d) -> p b d", b=NTB)
        HTH = sb("HTH", KT * T, F32R)[:].rearrange("p (k t) -> p k t", k=KT)
        HTL = sb("HTL", KT * T, F32R)[:].rearrange("p (k t) -> p k t", k=KT)
        REG = sb("REG", NK * T)
        RING = sb("RING", SLOTS * CF)[:].rearrange("p (s c) -> p s c", s=SLOTS)
        CH_ = sb("CARD_HIGH", SLOTS * CF, F32R)[:].rearrange("p (s c) -> p s c", s=SLOTS)
        CL_ = sb("CARD_LOW", SLOTS * CF, F32R)[:].rearrange("p (s c) -> p s c", s=SLOTS)
        WH = sb("WH", 2 * T, F32R)[:].rearrange("p (b t) -> p b t", b=2)
        WL = sb("WL", 2 * T, F32R)[:].rearrange("p (b t) -> p b t", b=2)
        SIDEB = sb("SIDEB", SIDE_F)
        FIX = sb("FIX", 2 * P)
        ROUTE = sb("ROUTE", 3 * T)[:].rearrange("p (a t) -> p a t", a=3)
        TINY = sb("TINY", 384)
        psum = ctx.enter_context(nc.psum_tensor("psum", [P, 8, 512], F32))

        ident = FIX[:, 0:P]
        iota = FIX[:, P:2 * P]

        def side(name):
            s, e = SIDE[name]
            return SIDEB[:, s:e]

        subk = side("subk").rearrange("p (c n) -> p c n", n=NK)
        wsmall = side("small").rearrange("p (k c) -> p k c", k=KT)

        at = [0]

        def reg(n):
            at[0] += n
            assert at[0] <= NK * T - 2 * KT * T
            return REG[:, at[0] - n:at[0]]

        mixc = reg(MC_F)

        def mc(name):
            s, e = MC[name]
            return mixc[:, s:e]

        XN = REG[:, NK * T - NTB * D:].rearrange("p (b d) -> p b d", b=NTB)
        HT = REG[:, NK * T - 2 * NTB * D:NK * T - NTB * D].rearrange("p (k t) -> p k t", k=KT)
        GFIN = REG[:, 0:D]
        QK = reg(14 * T).rearrange("p (c t) -> p c t", t=T)
        AQ, AK, BQ, BK, CQ, CK, DQ, DKEY = 0, 2, 4, 5, 6, 8, 10, 12
        VN = reg(NTB * NH * HV).rearrange("p (b h v) -> p b h v", b=NTB, h=NH)
        RN = reg(NTB * T).rearrange("p (b c) -> p b c", b=NTB)
        SIG = reg(NTB * T).rearrange("p (b c) -> p b c", b=NTB)
        GDT = reg(T)
        GLY, GLA_A, GLC, GLQ = reg(T), reg(T), reg(T), reg(T)
        FOXY, FOXA, FOXC = reg(T), reg(T), reg(T)
        KDEC = reg(CHOFF[NCH])
        PT = [reg(GH * KQ).rearrange("p (h c) -> p h c", h=GH) for _ in range(4)]
        scores_at = at[0]
        SA, SB_, SC, SD = [reg(GH * KQ).rearrange("p (h c) -> p h c", h=GH) for _ in range(4)]
        OALL = reg(NTB * NH * HV).rearrange("p (b h v) -> p b h v", b=NTB, h=NH)
        OSQ = REG[:, scores_at:scores_at + NTB * D].rearrange("p (b h v) -> p b h v", b=NTB, h=NH)
        OT = REG[:, scores_at + 2 * GH * KQ:scores_at + 2 * GH * KQ + KT * T].rearrange("p (k t) -> p k t", k=KT)
        ONRM = XN

        at[0] = EARLY * T
        QRY = reg(2 * HEADS * T).rearrange("p (c t) -> p c t", t=T)
        SCO = reg(NTB * 2 * HEADS * NK).rearrange("p (b c n) -> p b c n", b=NTB, n=NK)
        SCO2 = reg(2 * HEADS * NK).rearrange("p (c n) -> p c n", n=NK)
        CAND = reg(HEADS * 256).rearrange("p (h n) -> p h n", h=HEADS)
        CAND2 = reg(HEADS * 256).rearrange("p (h n) -> p h n", h=HEADS)
        PICK = reg(HEADS * 256).rearrange("p (h k a) -> p h k a", h=HEADS, k=TOPK)
        PICK2 = reg(HEADS * 256).rearrange("p (h k a) -> p h k a", h=HEADS, k=TOPK)
        TOPV = reg(2 * HK).rearrange("p (c k) -> p c k", k=TOPK)
        TOPI = reg(2 * HK).bitcast(U32).rearrange("p (c k) -> p c k", k=TOPK)
        TOPF = reg(2 * HK).rearrange("p (h c k) -> p h c k", c=2, k=TOPK)
        BEST = reg(HK).rearrange("p (h k) -> p h k", k=TOPK)
        POS = reg(HK).bitcast(U32).rearrange("p (h k) -> p h k", k=TOPK)
        POSA = reg(2 * HK).bitcast(U32).rearrange("p (c h k) -> p c h k", c=2, k=TOPK)
        POSF = reg(2 * HK).rearrange("p (c h k) -> p c h k", c=2, k=TOPK)
        CHOSEN = reg(NTB * 3 * HK).rearrange("p (b a c) -> p b a c", b=NTB, a=3)
        GSH = reg(NTB * HK).rearrange("p (b h k) -> p b h k", b=NTB, k=TOPK)
        G = REG[:, :].rearrange("p (j t) -> p j t", t=T)

        XF = X.rearrange("p b d -> p (b d)")
        OH = [t.rearrange("p (a t n) -> p a t n", a=2, t=4)
              for t in (XF[:, 0:D], XF[:, D:], SIDEB[:, 0:D], SIDEB[:, D:2 * D])]
        GEL = XF[:, 0:2 * T].rearrange("p (b t) -> p b t", b=2)

        SUMSQ, VAR, RS0, RT1 = TINY[:, 0:2], TINY[:, 2:4], TINY[:, 4:6], TINY[:, 6:8]
        RSTD = TINY[:, 8:10]
        RMID, NRMID = TINY[:, 16:16 + NCH], TINY[:, 24:24 + NCH]
        MAXN = TINY[:, 32:48].rearrange("p (g b h) -> p g b h", g=2, b=NTB)
        RDEN = TINY[:, 48:64].rearrange("p (b h) -> p b h", b=NTB)
        HSS, HVAR, HR0, HR1, HRS = [TINY[:, 64 + 32 * n:96 + 32 * n] for n in range(5)]
        GSUM = TINY[:, 256:272].rearrange("p (b h) -> p b h", b=NTB)
        GREC = TINY[:, 272:288].rearrange("p (b h) -> p b h", b=NTB)

        card_loaded = [sem(f"card_loaded{n}") for n in range(SLOTS)]
        high_ready = sem("high_ready")
        split_ready = sem("split_ready")
        card_used = sem("card_used")
        early_done = sem("early_done")
        early_read = sem("early_read")
        h_high = sem("h_high")
        h_low = sem("h_low")
        o_low = sem("o_low")
        o_high = sem("o_high")
        resid_in = sem("resid_in")
        start_loaded = sem("start_loaded")
        side_loaded = sem("side_loaded")
        mixc_loaded = sem("mixc_loaded")
        gfin_loaded = sem("gfin_loaded")
        sumsq_done = sem("sumsq_done")
        var_ready = sem("var_ready")
        rstd_rough = sem("rstd_rough")
        xn_ready = sem("xn_ready")
        xt_done = sem("xt_done")
        ht_ready = sem("ht_ready")
        small_done = sem("small_done")
        gd_ready = sem("gd_ready")
        gl_done = sem("gl_done")
        gly_ready = sem("gly_ready")
        gls_ready = sem("gls_ready")
        glc_ready = sem("glc_ready")
        gle_ready = sem("gle_ready")
        glq_ready = sem("glq_ready")
        foxy_ready = sem("foxy_ready")
        foxs_ready = sem("foxs_ready")
        foxc_ready = sem("foxc_ready")
        foxb_done = sem("foxb_done")
        foxb_read = sem("foxb_read")
        proj_read = sem("proj_read")
        r_exp = sem("r_exp")
        a_scores = sem("a_scores")
        a_soft = sem("a_soft")
        a_sp = sem("a_sp")
        a_tail = sem("a_tail")
        a_logw = sem("a_logw")
        a_exp = sem("a_exp")
        b_zeroed = sem("b_zeroed")
        b_scores = sem("b_scores")
        b_off = sem("b_off")
        c_scores = sem("c_scores")
        c_logits = sem("c_logits")
        c_exp = sem("c_exp")
        c_prob = sem("c_prob")
        c_flip = sem("c_flip")
        d_scores = sem("d_scores")
        d_logits = sem("d_logits")
        d_exp = sem("d_exp")
        d_flip = sem("d_flip")
        pt_ready = sem("pt_ready")
        pv_done = sem("pv_done")
        o_ready = sem("o_ready")
        o_scaled = sem("o_scaled")
        o_sq = sem("o_sq")
        hvar_ready = sem("hvar_ready")
        hrstd_rough = sem("hrstd_rough")
        onrm_ready = sem("onrm_ready")
        ot_done = sem("ot_done")
        ot_ready = sem("ot_ready")
        x_mixed = sem("x_mixed")
        pq_read = sem("pq_read")
        score_done = sem("score_done")
        score_read = sem("score_read")
        gate_shift = sem("gate_shift")
        gate_exp = sem("gate_exp")
        chosen_ready = sem("chosen_ready")
        route_done = sem("route_done")
        route_ready = sem("route_ready")
        onehot_equal = sem("onehot_equal")
        onehot_ready = sem("onehot_ready")
        gate_copied = sem("gate_copied")
        gate_done = sem("gate_done")
        gate_read = sem("gate_read")
        gelu_ready = sem("gelu_ready")
        wt_ready = sem("wt_ready")
        x_new = sem("x_new")
        y_ready = sem("y_ready")
        stored = sem("stored")

        block = ctx.enter_context(nc.Block())

        def split_of(m):
            return m if m < M_DENSE else m + EARLY

        @block.sync
        def _(sp):
            def load(l, first, r, slot):
                sp.dma_start(RING[:, slot, :], stream[l * CARDS + first + r * SLOTS + slot])\
                    .then_inc(card_loaded[slot], 16)

            with sp.Fori(0, DEPTH) as l:
                with sp.Fori(0, M_DENSE // SLOTS + 1) as r:
                    for slot in range(SLOTS):
                        sp.wait_ge(split_ready, l * SPLITS + r * SLOTS + slot + 1)
                        load(l, 0, r, slot)
                with sp.Fori(0, EARLY // SLOTS) as r:
                    for slot in range(SLOTS):
                        sp.wait_ge(early_done, l * EARLY + r * SLOTS + slot + 1)
                        load(l, M_DENSE + SLOTS, r, slot)
                with sp.Fori(0, (CARDS - M_DENSE - SLOTS - EARLY) // SLOTS) as r:
                    for slot in range(SLOTS):
                        sp.wait_ge(split_ready, l * SPLITS + SLOTS + M_DENSE + r * SLOTS + slot + 1)
                        load(l, M_DENSE + SLOTS + EARLY, r, slot)
            sp.wait_ge(y_ready, 1)
            sp.dma_start(out.rearrange("a (b p) d -> p (a b) d", p=P), XN).then_inc(stored, 16)
            sp.wait_ge(stored, 16)

        @block.gpsimd
        def _(pool):
            with pool.Fori(0, DEPTH) as l:
                with pool.Fori(0, GROUPS // 4) as r:
                    for s in range(4):
                        pool.wait_ge(onehot_equal, l * GROUPS + r * 4 + s + 1)
                        gates = ROUTE[:, 2, bass.ds(r * 16 + s * 4, 4)].unsqueeze(2).to_broadcast([P, 4, NK])
                        pool.tensor_tensor(OH[s][:, 0], OH[s][:, 0], gates, ALU.mult).then_inc(onehot_ready, 1)

        @block.scalar
        def _(act):
            def rough_rsqrt(dst, tmp, src):
                act.activation(tmp, src, ACT.Ln)
                act.drain()
                return act.activation(dst, tmp, ACT.Exp, scale=-0.5)

            def norm_stats(n):
                for b in range(NTB):
                    last = act.activation(XN[:, b, :], X[:, b, :], ACT.Square, accum_out=SUMSQ[:, b:b + 1])
                last.then_inc(sumsq_done, 1)
                act.wait_ge(var_ready, n + 1)
                rough_rsqrt(RS0, RT1, VAR).then_inc(rstd_rough, 1)

            def softplus_tail(dst, src):
                act.activation(dst, src, ACT.Abs)
                act.drain()
                act.activation(dst, dst, ACT.Exp, scale=-1.0)
                act.drain()
                return act.activation(dst, dst, ACT.Ln, bias=1.0)

            def high(l, m, r=0):
                n = split_of(m)
                act.wait_ge(card_loaded[n % SLOTS], l * (16 * CARDS // SLOTS) + 16 * (n // SLOTS) + 16 * r + 16)
                if m >= SLOTS:
                    act.wait_ge(card_used, l * SPLITS + m - SLOTS + 1 + SLOTS * r)
                act.copy(CH_[:, m % SLOTS, :], RING[:, n % SLOTS, :]).then_inc(high_ready, 1)

            act.dma_start(X, x_in.rearrange("a (b p) d -> p (a b) d", p=P)).then_inc(start_loaded, 16)
            act.dma_start(FIX[:, :], fixed_in).then_inc(start_loaded, 16)
            act.wait_ge(start_loaded, 32)
            with act.Fori(0, DEPTH) as l:
                act.wait_ge(x_new, l * 4)
                act.dma_start(SIDEB[:, :], side_in[l]).then_inc(side_loaded, 16)
                act.dma_start(mixc, mixc_in).then_inc(mixc_loaded, 16)
                norm_stats(l * 2)
                for m in range(3):
                    high(l, m)
                act.wait_ge(ht_ready, l * 8 + 4)
                act.copy(HTH, HT).then_inc(h_high, 1)
                act.wait_ge(small_done, l + 1)
                act.copy(GDT[0:RANK, :], psum[0:RANK, 7, 0:T]).then_inc(gd_ready, 1)
                for c in range(C_IN):
                    high(l, c + 3)
                    if c == 4:
                        act.wait_ge(gly_ready, l + 1)
                        softplus_tail(GLA_A, GLY).then_inc(gls_ready, 1)
                        act.wait_ge(foxy_ready, l + 1)
                        softplus_tail(FOXA[FOX0:SMALL, :], FOXY[FOX0:SMALL, :]).then_inc(foxs_ready, 1)
                    act.wait_ge(card_used, l * SPLITS + c + 1)
                    if c < IN_T:
                        act.activation(QK[:, c, :], psum[:, c % 4, 0:T], ACT.Copy,
                                       scale=0.125 if c in (0, 1, 6, 7, 10, 11) else 1.0).then_inc(proj_read, 1)
                    elif c % 2:
                        if c == IN_T + 1:
                            act.wait_ge(b_zeroed, l + 1)
                        p = (c - IN_T) // 2
                        for b in range(NTB):
                            src = psum[:, 4 + 2 * (p % 2) + b, 0:T]
                            if p < 4:
                                last = act.copy(VN[:, b, GH * p:GH * p + GH, 0:HD],
                                                src.rearrange("p (h v) -> p h v", h=GH))
                            else:
                                last = act.copy(RN[:, b, :], src)
                        last.then_inc(proj_read, 1)
                act.drain()
                act.activation(SIG[:, :, :], RN[:, :, :], ACT.Exp, scale=-1.0).then_inc(r_exp, 1)
                act.wait_ge(glc_ready, l + 1)
                for c in range(NCH):
                    act.activation(KDEC[:, CHOFF[c]:CHOFF[c + 1]], GLC[:, 0:CH * (c + 1)], ACT.Exp,
                                   bias=NRMID[:, c:c + 1], scale=1.0 / TAU)
                act.activation(GLQ, GLQ, ACT.Exp, scale=-1.0 / TAU).then_inc(gle_ready, 1)
                act.wait_ge(a_scores, l + 1)
                softplus_tail(SA[:, :, :], psum[:, 0:GH, 0:KQ]).then_inc(a_soft, 1)
                act.wait_ge(c_logits, l + 1)
                for b in range(NTB):
                    for h in range(GH):
                        cols = slice(0, P) if b == 0 else slice(P, KQ)
                        last = act.activation(SC[:, h, cols], SC[:, h, cols], ACT.Exp, bias=MAXN[:, 0, b, h:h + 1])
                last.then_inc(c_exp, 1)
                act.wait_ge(a_logw, l + 1)
                act.activation(PT[0][:, :, :], SA[:, :, :], ACT.Exp).then_inc(a_exp, 1)
                act.wait_ge(c_flip, l + 1)
                act.copy(PT[2][:, :, :], psum[:, GH:2 * GH, 0:KQ]).then_inc(pt_ready, 1)
                act.wait_ge(b_scores, l + 1)
                act.copy(PT[1][:, :, P:2 * P], psum[:, 0:GH, P:2 * P]).then_inc(b_off, 1)
                act.wait_ge(d_logits, l + 1)
                for b in range(NTB):
                    for h in range(GH):
                        cols = slice(0, P) if b == 0 else slice(P, KQ)
                        last = act.activation(SD[:, h, cols], SD[:, h, cols], ACT.Exp, bias=MAXN[:, 1, b, h:h + 1])
                last.then_inc(d_exp, 1)
                act.wait_ge(d_flip, l + 1)
                act.copy(PT[3][:, :, :], psum[:, GH:2 * GH, 0:KQ]).then_inc(pt_ready, 1)
                act.wait_ge(o_scaled, l + 1)
                act.activation(OSQ[:, :, :, :], OALL[:, :, :, 0:HD], ACT.Square).then_inc(o_sq, 1)
                act.wait_ge(hvar_ready, l + 1)
                rough_rsqrt(HR0, HR1, HVAR).then_inc(hrstd_rough, 1)
                act.wait_ge(ot_ready, l * 4 + 4)
                act.copy(HTH, OT).then_inc(o_high, 1)
                for u in range(C_OUT):
                    high(l, M_OUT + u + 3)
                act.wait_ge(card_used, l * SPLITS + M_PQ)
                for n in range(4):
                    last = act.copy(X[:, n // 2, (n % 2) * 512:(n % 2 + 1) * 512], psum[:, n, :])
                last.then_inc(x_mixed, 1)
                act.drain()
                norm_stats(l * 2 + 1)
                act.wait_ge(ht_ready, l * 8 + 8)
                act.copy(HTH, HT).then_inc(h_high, 1)
                for c in range(C_PQ):
                    if M_PQ + c + 3 < M_DENSE:
                        high(l, M_PQ + c + 3)
                    act.wait_ge(card_used, l * SPLITS + M_PQ + c + 1)
                    act.copy(QRY[:, c, :], psum[:, c % 4, 0:T]).then_inc(pq_read, 1)
                for b in range(NTB):
                    for n in range(2):
                        act.wait_ge(score_done, l * 2 * NTB + 2 * b + n + 1)
                        act.copy(SCO[:, b, 8 * n:8 * n + 8, :], psum[:, 4 + 2 * n:6 + 2 * n, :]
                                 .rearrange("p b (c n) -> p (b c) n", n=NK)).then_inc(score_read, 1)
                with act.Fori(0, EARLY // 4) as r:
                    for s in range(4):
                        act.wait_ge(early_done, l * EARLY + r * 4 + s + 1)
                        act.activation(G[:, bass.ds(r * 4 + s, 1), :], psum[:, 4 + s % 2, 0:T].unsqueeze(1),
                                       ACT.Gelu).then_inc(early_read, 1)
                act.wait_ge(gate_shift, l + 1)
                act.activation(GSH[:, :, :, :], GSH[:, :, :, :], ACT.Exp).then_inc(gate_exp, 1)
                high(l, M_DENSE)
                high(l, M_DENSE + 1)
                with act.Fori(0, GROUPS // 4) as r:
                    for s in range(4):
                        act.wait_ge(gate_done, l * GROUPS + r * 4 + s + 1)
                        act.copy(G[:, EARLY:, bass.ds(r * 16 + s * 4, 4)],
                                 psum[:, 4 + s, :].rearrange("p (t j) -> p j t", t=4)[:, EARLY:, :])\
                            .then_inc(gate_copied, 1)
                with act.Fori(0, EARLY // 4) as r:
                    for s in range(4):
                        high(l, M_DENSE + 2 + s, r)
                high(l, M_STEP + 1)

                def gelu_late(n, used, a):
                    act.wait_ge(card_used, l * SPLITS + used)
                    act.wait_ge(wt_ready, l * NK + EARLY + n - 1)
                    act.activation(GEL[:, a, :], psum[:, 4 + a, 0:T], ACT.Gelu).then_inc(gelu_ready, 1)

                gelu_late(0, M_FIRST + 1, 0)
                with act.Fori(0, STEP_PAIRS) as r:
                    for s in range(2):
                        high(l, M_STEP + 2 + 2 * s, r)
                        high(l, M_STEP + 3 + 2 * s, r)
                        gelu_late(r * 2 + s + 1, M_STEP + 1 + 2 * s + r * 4, (s + 1) % 2)
                high(l, SPLITS - 1)
                gelu_late(LATE - 1, SPLITS - 2, 1)
                act.wait_ge(card_used, l * SPLITS + SPLITS)
                for n in range(4):
                    act.copy(X[:, n // 2, (n % 2) * 512:(n % 2 + 1) * 512], psum[:, n, :]).then_inc(x_new, 1)
                act.drain()
            act.dma_start(GFIN, gfin_in).then_inc(gfin_loaded, 16)
            norm_stats(DEPTH * 2)

        @block.vector
        def _(dve):
            def refine_rsqrt(dst, tmp, rough, var):
                dve.tensor_tensor(tmp, rough, rough, ALU.mult)
                dve.drain()
                dve.tensor_tensor(tmp, tmp, var, ALU.mult)
                dve.drain()
                dve.tensor_scalar(tmp, tmp, -0.5, 1.5, ALU.mult, ALU.add)
                dve.drain()
                dve.tensor_tensor(dst, rough, tmp, ALU.mult)
                dve.drain()

            def norm_rstd(n):
                dve.wait_ge(sumsq_done, n + 1)
                dve.tensor_scalar(VAR, SUMSQ, 1.0 / D, EPS, ALU.mult, ALU.add).then_inc(var_ready, 1)
                dve.wait_ge(rstd_rough, n + 1)
                refine_rsqrt(RSTD, RT1, RS0, VAR)

            def low(l, m, r=0):
                n = split_of(m)
                dve.wait_ge(high_ready, l * SPLITS + m + 1 + SLOTS * r)
                dve.tensor_tensor(CL_[:, m % SLOTS, :], RING[:, n % SLOTS, :], CH_[:, m % SLOTS, :].bitcast(F32),
                                  ALU.subtract).then_inc(split_ready, 1)

            def scaled_transpose(dst, done, n, gain):
                for m in range(4):
                    dve.wait_ge(done, n * 4 + m + 1)
                    half = m % 2
                    last = dve.tensor_tensor(dst[:, 4 * half:4 * half + 4, (m // 2) * P:(m // 2 + 1) * P],
                                             psum[:, m, :].rearrange("p (k t) -> p k t", k=4),
                                             gain[:, 4 * half:4 * half + 4].unsqueeze(2).to_broadcast([P, 4, P]),
                                             ALU.mult)
                    if done is xt_done:
                        last.then_inc(ht_ready, 1)
                    else:
                        last.then_inc(ot_ready, 1)

            def norm(n, gain):
                norm_rstd(n)
                for b in range(NTB):
                    dve.tensor_scalar(XN[:, b, :], X[:, b, :], RSTD[:, b:b + 1], None, ALU.mult).then_inc(xn_ready, 1)
                scaled_transpose(HT, xt_done, n, gain)

            def norm_low(n):
                dve.wait_ge(h_high, n + 1)
                dve.tensor_tensor(HTL, HT, HTH.bitcast(F32), ALU.subtract).then_inc(h_low, 1)

            def diagonal(t):
                return t.rearrange("p h (b q) -> p h b q", b=3)[:, :, 0:3:2, :]

            def masked(t, src, name):
                m = mc(name).unsqueeze(1).to_broadcast([P, 2, P]).unsqueeze(1).to_broadcast([P, GH, 2, P])
                return dve.tensor_tensor(diagonal(t), diagonal(src), m, ALU.mult)

            def row_max(src, g):
                dve.tensor_reduce(MAXN[:, g, 0, :], src[:, :, 0:P], AX.X, ALU.max)
                dve.tensor_reduce(MAXN[:, g, 1, :], src[:, :, P:KQ], AX.X, ALU.max)
                dve.drain()
                return dve.tensor_scalar(MAXN[:, g, :, :], MAXN[:, g, :, :], -1.0, None, ALU.mult)

            def take_o(l, g, bank, order):
                dve.wait_ge(pv_done, l * 4 + order)
                for b in range(NTB):
                    last = dve.tensor_copy(OALL[:, b, GH * g:GH * g + GH, :],
                                           psum[:, bank + b, 0:GH * HV].rearrange("p (h v) -> p h v", h=GH))
                last.then_inc(o_ready, 1)

            dve.memset(TINY[:, 380:384], 0.0).then_inc(split_ready, SLOTS)
            dve.wait_ge(start_loaded, 32)
            with dve.Fori(0, DEPTH) as l:
                dve.wait_ge(x_new, l * 4)
                dve.memset(PT[1][:, :, :], 0.0)
                dve.memset(VN[:, :, :, HD:HV], 1.0).then_inc(b_zeroed, 1)
                dve.wait_ge(side_loaded, l * 16 + 16)
                dve.wait_ge(mixc_loaded, l * 16 + 16)
                norm(l * 2, side("g_mix"))
                for m in range(3):
                    low(l, m)
                norm_low(l * 2)
                low(l, 3)
                dve.wait_ge(small_done, l + 1)
                dve.tensor_scalar(FOXY[FOX0:SMALL, :], psum[FOX0:SMALL, 7, 0:T],
                                  side("b_fox")[FOX0:SMALL, :], -1.0, ALU.add, ALU.mult).then_inc(foxy_ready, 1)
                dve.wait_ge(gl_done, l + 1)
                dve.tensor_scalar(GLY, psum[:, 6, 0:T], side("b_gla"), -1.0, ALU.add, ALU.mult).then_inc(gly_ready, 1)
                for m in range(4, 8):
                    low(l, m)
                dve.wait_ge(gls_ready, l + 1)
                dve.scalar_tensor_tensor(GLA_A, GLY, 0.0, GLA_A, ALU.max, ALU.add)
                dve.drain()
                dve.tensor_tensor_scan(GLC, mc("ones"), GLA_A, 0.0, ALU.mult, ALU.add)
                dve.drain()
                mid = GLC.rearrange("p (c s) -> p c s", s=CH)[:, :, CH // 2 - 1:CH // 2]
                dve.tensor_scalar(NRMID.unsqueeze(2), mid, -1.0 / TAU, None, ALU.mult)
                dve.tensor_tensor(GLQ.rearrange("p (c s) -> p c s", s=CH), GLC.rearrange("p (c s) -> p c s", s=CH),
                                  mid.to_broadcast([P, NCH, CH]), ALU.subtract).then_inc(glc_ready, 1)
                dve.wait_ge(foxs_ready, l + 1)
                rows = slice(FOX0, SMALL)
                dve.scalar_tensor_tensor(FOXA[rows, :], FOXY[rows, :], 0.0, FOXA[rows, :], ALU.max, ALU.add)
                dve.drain()
                dve.tensor_tensor_scan(FOXC[rows, :], mc("ones")[rows, :], FOXA[rows, :], 0.0,
                                       ALU.mult, ALU.add).then_inc(foxc_ready, 1)
                for m in range(8, C_IN + 3):
                    low(l, m)
                dve.wait_ge(r_exp, l + 1)
                dve.tensor_scalar(SIG[:, :, :], SIG[:, :, :], 1.0, None, ALU.add)
                dve.drain()
                dve.reciprocal(SIG[:, :, :], SIG[:, :, :])
                dve.drain()
                dve.tensor_tensor(SIG[:, :, :], SIG[:, :, :], RN[:, :, :], ALU.mult)
                dve.wait_ge(gle_ready, l + 1)
                dve.wait_ge(proj_read, l * (IN_T + 5) + 6)
                dve.scalar_tensor_tensor(GLQ, GLQ, DK ** -0.5, QK[:, BQ, :], ALU.mult, ALU.mult)
                for c in range(NCH):
                    last = dve.tensor_tensor(KDEC[:, CHOFF[c]:CHOFF[c + 1]], KDEC[:, CHOFF[c]:CHOFF[c + 1]],
                                             QK[:, BK, 0:CH * (c + 1)], ALU.mult)
                last.then_inc(glq_ready, 1)
                dve.wait_ge(foxb_done, l + 1)
                for h in range(GH):
                    fb = psum[:, 4 + h, :]
                    dve.tensor_tensor(SD[:, h, 0:P], fb[:, 0:P], mc("fox_mask")[:, 0:P], ALU.add)
                    last = dve.tensor_tensor(SD[:, h, P:KQ], fb[:, 0:T], mc("fox_mask")[:, P:KQ], ALU.add)
                last.then_inc(foxb_read, 1)
                dve.wait_ge(c_scores, l + 1)
                dve.tensor_tensor(SC[:, :, :], psum[:, GH:2 * GH, 0:KQ],
                                  mc("dil_bias").rearrange("p (h c) -> p h c", h=GH), ALU.add)
                dve.drain()
                row_max(SC, 0).then_inc(c_logits, 1)
                dve.wait_ge(a_soft, l + 1)
                dve.scalar_tensor_tensor(SA[:, :, :], psum[:, 0:GH, 0:KQ], 0.0, SA[:, :, :], ALU.max, ALU.add)
                dve.drain()
                dve.tensor_tensor(SB_[:, :, :], psum[:, 0:GH, 0:KQ], SA[:, :, :], ALU.subtract)
                dve.drain()
                masked(SA, SA, "k_lt_q").then_inc(a_sp, 1)
                dve.wait_ge(c_exp, l + 1)
                dve.tensor_tensor(SC[:, :, :], SC[:, :, :],
                                  mc("dil_count").unsqueeze(1).to_broadcast([P, GH, KQ]), ALU.mult).then_inc(c_prob, 1)
                dve.wait_ge(a_tail, l + 1)
                dve.tensor_tensor(SA[:, :, :], SB_[:, :, :], psum[:, 0:GH, 0:KQ], ALU.subtract).then_inc(a_logw, 1)
                dve.wait_ge(a_exp, l + 1)
                masked(PT[0], PT[0], "k_lt_q").then_inc(pt_ready, 1)
                take_o(l, 0, 0, 1)
                take_o(l, 2, 4, 2)
                dve.wait_ge(b_off, l + 1)
                for m in range(4):
                    r = CH * (m + 1)
                    cols = slice(CH * m, CH * m + CH)
                    mask = mc("k_le_q")[0:r, cols].unsqueeze(1).to_broadcast([r, 2, CH]).unsqueeze(1)\
                        .to_broadcast([r, GH, 2, CH])
                    last = dve.tensor_tensor(diagonal(PT[1])[0:r, :, :, cols],
                                             diagonal(psum[:, 0:GH, 0:KQ])[0:r, :, :, cols], mask, ALU.mult)
                last.then_inc(pt_ready, 1)
                dve.wait_ge(d_scores, l + 1)
                dve.tensor_tensor(SD[:, :, :], psum[:, GH:2 * GH, 0:KQ], SD[:, :, :], ALU.add)
                dve.drain()
                row_max(SD, 1).then_inc(d_logits, 1)
                take_o(l, 1, 0, 3)
                take_o(l, 3, 4, 4)
                dve.drain()
                dve.reciprocal(RDEN, OALL[:, :, 2 * GH:, HD])
                dve.drain()
                dve.tensor_tensor(OALL[:, :, 2 * GH:, 0:HD], OALL[:, :, 2 * GH:, 0:HD],
                                  RDEN.unsqueeze(3).to_broadcast([P, NTB, 2 * GH, HD]), ALU.mult).then_inc(o_scaled, 1)
                dve.wait_ge(o_sq, l + 1)
                dve.tensor_reduce(HSS.rearrange("p (b h) -> p b h", b=NTB), OSQ[:, :, :, :], AX.X, ALU.add)
                dve.drain()
                dve.tensor_scalar(HVAR, HSS, 1.0 / HD, EPS, ALU.mult, ALU.add).then_inc(hvar_ready, 1)
                dve.wait_ge(hrstd_rough, l + 1)
                refine_rsqrt(HRS, HR1, HR0, HVAR)
                onrm = ONRM.rearrange("p b (h v) -> p b h v", h=NH)
                dve.tensor_tensor(onrm, OALL[:, :, :, 0:HD], HRS.rearrange("p (b h) -> p b h", b=NTB).unsqueeze(3)
                                  .to_broadcast([P, NTB, NH, HD]), ALU.mult)
                dve.drain()
                dve.tensor_tensor(ONRM[:, :, T:2 * T], ONRM[:, :, T:2 * T], SIG[:, :, :], ALU.mult).then_inc(onrm_ready, 1)
                scaled_transpose(OT, ot_done, l, side("g_head"))
                dve.wait_ge(o_high, l + 1)
                dve.tensor_tensor(HTL, OT, HTH.bitcast(F32), ALU.subtract).then_inc(o_low, 1)
                for u in range(C_OUT):
                    low(l, M_OUT + u + 3)
                norm(l * 2 + 1, side("g_ffn"))
                norm_low(l * 2 + 1)
                for m in range(M_PQ + 3, M_DENSE):
                    low(l, m)
                for b in range(NTB):
                    dve.wait_ge(score_read, l * 2 * NTB + 2 * b + 2)
                    dve.memset(GREC, 0.0)
                    for c in range(2 * HEADS):
                        dve.max(TOPV[:, c, 0:8], SCO[:, b, c, :])
                    dve.drain()
                    for c in range(2 * HEADS):
                        dve.max_index(TOPI[:, c, 0:8], TOPV[:, c, 0:8], SCO[:, b, c, :])
                        dve.match_replace(SCO2[:, c, :], TOPV[:, c, 0:8], SCO[:, b, c, :], LOWEST)
                    dve.drain()
                    for c in range(2 * HEADS):
                        dve.max(TOPV[:, c, 8:16], SCO2[:, c, :])
                    dve.drain()
                    for c in range(2 * HEADS):
                        dve.max_index(TOPI[:, c, 8:16], TOPV[:, c, 8:16], SCO2[:, c, :])
                    v = TOPV.rearrange("p (h c) k -> p h c k", c=2)
                    dve.tensor_tensor(CAND.rearrange("p h (a b) -> p h a b", a=TOPK),
                                      v[:, :, 0, :].unsqueeze(3).to_broadcast([P, HEADS, TOPK, TOPK]),
                                      v[:, :, 1, :].unsqueeze(2).to_broadcast([P, HEADS, TOPK, TOPK]), ALU.add)
                    dve.drain()
                    dve.tensor_copy(TOPF, TOPI.rearrange("p (h c) k -> p h c k", c=2))
                    for h in range(HEADS):
                        dve.max(BEST[:, h, 0:8], CAND[:, h, :])
                    dve.drain()
                    for h in range(HEADS):
                        dve.max_index(POS[:, h, 0:8], BEST[:, h, 0:8], CAND[:, h, :])
                        dve.match_replace(CAND2[:, h, :], BEST[:, h, 0:8], CAND[:, h, :], LOWEST)
                    dve.drain()
                    for h in range(HEADS):
                        dve.max(BEST[:, h, 8:16], CAND2[:, h, :])
                    dve.drain()
                    for h in range(HEADS):
                        dve.max_index(POS[:, h, 8:16], BEST[:, h, 8:16], CAND2[:, h, :])
                    last = dve.tensor_tensor(GSH[:, b], BEST, BEST[:, :, 0:1].to_broadcast([P, HEADS, TOPK]),
                                             ALU.subtract)
                    if b == NTB - 1:
                        last.then_inc(gate_shift, 1)
                    dve.drain()
                    dve.tensor_scalar(POSA[:, 0], POS, 4, None, ALU.logical_shift_right)
                    dve.tensor_scalar(POSA[:, 1], POS, TOPK - 1, None, ALU.bitwise_and)
                    dve.drain()
                    dve.tensor_copy(POSF, POSA)
                    dve.drain()
                    small_iota = iota[:, 0:TOPK].unsqueeze(1).to_broadcast([P, TOPK, TOPK]).unsqueeze(1)\
                        .to_broadcast([P, HEADS, TOPK, TOPK])
                    for c, pick in ((0, PICK), (1, PICK2)):
                        dve.tensor_tensor(pick, POSF[:, c].unsqueeze(3).to_broadcast([P, HEADS, TOPK, TOPK]),
                                          small_iota, ALU.is_equal)
                    dve.drain()
                    for c, pick in ((0, PICK), (1, PICK2)):
                        dve.tensor_tensor(pick, pick, TOPF[:, :, c, :].unsqueeze(2)
                                          .to_broadcast([P, HEADS, TOPK, TOPK]), ALU.mult)
                    dve.drain()
                    for c, pick in ((0, PICK), (1, PICK2)):
                        dve.tensor_reduce(CHOSEN[:, b, c, :].rearrange("p (h k) -> p h k", h=HEADS), pick, AX.X, ALU.add)
                dve.wait_ge(gate_exp, l + 1)
                dve.tensor_reduce(GSUM, GSH, AX.X, ALU.add)
                dve.drain()
                dve.reciprocal(GREC, GSUM)
                dve.drain()
                dve.tensor_tensor(CHOSEN[:, :, 2, :].rearrange("p b (h k) -> p b h k", h=HEADS), GSH,
                                  GREC.unsqueeze(3).to_broadcast([P, NTB, HEADS, TOPK]), ALU.mult).then_inc(chosen_ready, 1)
                low(l, M_DENSE)
                low(l, M_DENSE + 1)
                for b in range(NTB):
                    dve.wait_ge(route_done, l * NTB + b + 1)
                    last = dve.tensor_copy(ROUTE[:, :, b * P:(b + 1) * P],
                                           psum[:, 6 + b, 0:3 * P].rearrange("p (a t) -> p a t", a=3))
                last.then_inc(route_ready, 1)
                dve.drain()
                dve.wait_ge(resid_in, l + 1)

                def onehot_rows(first, s):
                    tok = ROUTE[:, 0:2, bass.ds(first, 4)].unsqueeze(3).to_broadcast([P, 2, 4, NK])
                    numbers = iota.unsqueeze(1).to_broadcast([P, 4, NK]).unsqueeze(1).to_broadcast([P, 2, 4, NK])
                    dve.tensor_tensor(OH[s], numbers, tok, ALU.is_equal).then_inc(onehot_equal, 1)

                def early_weights(r, s):
                    dve.wait_ge(gate_copied, l * GROUPS + r * 4 + s + 1)
                    cols = G[:, 0:EARLY, bass.ds(r * 16 + s * 4, 4)]
                    dve.tensor_tensor(cols, psum[:, 4 + s, :].rearrange("p (t j) -> p j t", t=4)[:, 0:EARLY, :],
                                      cols, ALU.mult).then_inc(gate_read, 1)

                onehot_rows(0, 0)
                onehot_rows(4, 1)
                with dve.Fori(0, GROUPS // 4 - 1) as r:
                    for s in range(4):
                        onehot_rows(r * 16 + 4 * s + 8, (s + 2) % 4)
                        early_weights(r, s)
                for s in range(4):
                    if s < 2:
                        onehot_rows(T - 8 + 4 * s, s + 2)
                    early_weights(GROUPS // 4 - 1, s)
                dve.drain()

                def weigh(col, a, used, gelu):
                    wj = G[:, bass.ds(col, 1), :]
                    if gelu is not None:
                        dve.wait_ge(gelu_ready, l * LATE + gelu)
                        dve.tensor_tensor(wj, GEL[:, a, :].unsqueeze(1), wj, ALU.mult)
                        dve.drain()
                    dve.wait_ge(card_used, l * SPLITS + used)
                    dve.tensor_scalar(WH[:, a, :].unsqueeze(1), wj, 1.0, None, ALU.mult)
                    dve.drain()
                    dve.tensor_tensor(WL[:, a, :].unsqueeze(1), wj, WH[:, a, :].bitcast(F32).unsqueeze(1),
                                      ALU.subtract).then_inc(wt_ready, 1)

                with dve.Fori(0, EARLY // 4) as r:
                    for s in range(4):
                        low(l, M_DENSE + 2 + s, r)
                        weigh(r * 4 + s, s % 2, M_DENSE + s - 1 + r * 4, None)
                low(l, M_STEP + 1)
                weigh(EARLY, 0, M_FIRST - 1, 1)
                with dve.Fori(0, STEP_PAIRS) as r:
                    for s in range(2):
                        low(l, M_STEP + 2 + 2 * s, r)
                        low(l, M_STEP + 3 + 2 * s, r)
                        weigh(r * 2 + EARLY + s + 1, (s + 1) % 2, M_STEP + 2 * s + r * 4, r * 2 + s + 2)
                low(l, SPLITS - 1)
                weigh(NK - 1, 1, SPLITS - 3, LATE)
            norm_rstd(DEPTH * 2)
            dve.wait_ge(gfin_loaded, 16)
            for b in range(NTB):
                last = dve.scalar_tensor_tensor(XN[:, b, :], X[:, b, :], RSTD[:, b:b + 1], GFIN, ALU.mult, ALU.mult)
            last.then_inc(y_ready, 1)

        @block.tensor
        def _(pe):
            def card(l, m, r=0):
                pe.wait_ge(split_ready, SLOTS + l * SPLITS + m + 1 + SLOTS * r)
                return CH_[:, m % SLOTS, :], CL_[:, m % SLOTS, :]

            def product(out, wh, wl, xh, xl, start, stop):
                pe.matmul(out, wh, xh, start=start, stop=False)
                pe.matmul(out, wh, xl, start=False, stop=False)
                return pe.matmul(out, wl, xh, start=False, stop=stop)

            def flip_norm(n):
                for m in range(4):
                    if m % 2 == 0:
                        pe.wait_ge(xn_ready, n * 2 + m // 2 + 1)
                    for k in range(4):
                        last = pe.transpose(psum[:, m, k * P:(k + 1) * P],
                                            XN[:, m // 2, (4 * (m % 2) + k) * P:(4 * (m % 2) + k + 1) * P], ident)
                    last.then_inc(xt_done, 1)

            def columns_first(l, m, bank, r=0):
                wh, wl = [w.rearrange("p (k c) -> p k c", k=KT) for w in card(l, m, r)]
                for k in range(KT):
                    last = product(psum[:, bank, 0:T], wh[:, k, :], wl[:, k, :], HTH[:, k, :], HTL[:, k, :],
                                   k == 0, k == KT - 1)
                last.then_inc(card_used, 1)

            def pv(g, bank):
                for b in range(NTB):
                    for h in range(GH):
                        o = psum[:, bank + b, h * HV:(h + 1) * HV]
                        if b == 0:
                            last = pe.matmul(o, PT[g][:, h, 0:P], VN[:, 0, GH * g + h, :], start=True, stop=True)
                        else:
                            pe.matmul(o, PT[g][:, h, P:2 * P], VN[:, 0, GH * g + h, :], start=True, stop=False)
                            last = pe.matmul(o, PT[g][:, h, 2 * P:KQ], VN[:, 1, GH * g + h, :], start=False, stop=True)
                last.then_inc(pv_done, 1)

            def qk_scores(q, k, bank):
                for h in range(GH):
                    rows = slice(HD * (h % 2), HD * (h % 2) + HD)
                    qT, kT = QK[rows, q + h // 2, :], QK[rows, k + h // 2, :]
                    pe.matmul(psum[:, bank + h, 0:P], qT[:, 0:P], kT[:, 0:P], start=True, stop=True)
                    last = pe.matmul(psum[:, bank + h, P:KQ], qT[:, P:T], kT[:, 0:T], start=True, stop=True)
                return last

            def flip(src, bank):
                for h in range(GH):
                    for n in range(3):
                        last = pe.transpose(psum[:, bank + h, n * P:(n + 1) * P], src[:, h, n * P:(n + 1) * P], ident)
                return last

            pe.wait_ge(start_loaded, 32)
            with pe.Fori(0, DEPTH) as l:
                pe.wait_ge(side_loaded, l * 16 + 16)
                flip_norm(l * 2)
                pe.wait_ge(ht_ready, l * 8 + 4)
                for k in range(KT):
                    last = pe.matmul(psum[0:SMALL, 7, 0:T], wsmall[:, k, :], HT[:, k, :], start=(k == 0), stop=(k == KT - 1))
                last.then_inc(small_done, 1)
                pe.wait_ge(h_low, l * 2 + 1)
                for c in range(C_IN):
                    if c == 2:
                        pe.wait_ge(gd_ready, l + 1)
                        pe.matmul(psum[:, 6, 0:T], side("up")[0:RANK, :], GDT[0:RANK, :], start=True, stop=True).then_inc(gl_done, 1)
                    if c < IN_T:
                        if c >= 4:
                            pe.wait_ge(proj_read, l * (IN_T + 5) + c - 3)
                        columns_first(l, c, c % 4)
                    else:
                        p, half = (c - IN_T) // 2, (c - IN_T) % 2
                        if half == 0 and p < 2:
                            pe.wait_ge(gly_ready, l + 1)
                        elif half == 0:
                            pe.wait_ge(proj_read, l * (IN_T + 5) + IN_T + p - 1)
                        wh, wl = [w.rearrange("p (k c) -> p k c", k=4) for w in card(l, c)]
                        for b in range(NTB):
                            for k in range(4):
                                kk, tb = 4 * half + k, slice(b * P, (b + 1) * P)
                                last = product(psum[:, 4 + 2 * (p % 2) + b, 0:T], HTH[:, kk, tb], HTL[:, kk, tb],
                                               wh[:, k, :], wl[:, k, :], kk == 0, kk == KT - 1)
                        last.then_inc(card_used, 1)
                pe.wait_ge(foxc_ready, l + 1)
                pe.wait_ge(proj_read, l * (IN_T + 5) + IN_T + 5)
                for h in range(GH):
                    last = pe.matmul(psum[:, 4 + h, 0:T], mc("head_sel")[FOX0:SMALL, h * P:(h + 1) * P],
                                     FOXC[FOX0:SMALL, :], start=True, stop=True)
                last.then_inc(foxb_done, 1)
                for h in range(GH):
                    rows = slice(HD * (h % 2), HD * (h % 2) + HD)
                    qT, kT = QK[rows, AQ + h // 2, :], QK[rows, AK + h // 2, :]
                    pe.matmul(psum[:, h, 0:T], kT[:, 0:P], qT[:, 0:T], start=True, stop=True)
                    last = pe.matmul(psum[:, h, T:KQ], kT[:, P:T], qT[:, P:T], start=True, stop=True)
                last.then_inc(a_scores, 1)
                pe.wait_ge(foxb_read, l + 1)
                qk_scores(CQ, CK, GH).then_inc(c_scores, 1)
                pe.wait_ge(a_sp, l + 1)
                for h in range(GH):
                    pe.matmul(psum[:, h, 0:T], mc("tri"), SA[:, h, 0:T], start=True, stop=False)
                    pe.matmul(psum[:, h, P:T], mc("ones")[:, 0:P], SA[:, h, T:KQ], start=False, stop=True)
                    last = pe.matmul(psum[:, h, T:KQ], mc("tri"), SA[:, h, T:KQ], start=True, stop=True)
                last.then_inc(a_tail, 1)
                pe.wait_ge(c_prob, l + 1)
                flip(SC, GH).then_inc(c_flip, 1)
                pe.wait_ge(pt_ready, l * 4 + 2)
                pv(0, 0)
                pv(2, 4)
                pe.wait_ge(o_ready, l * 4 + 1)
                pe.wait_ge(glq_ready, l + 1)
                for h in range(GH):
                    rows = slice(DK * h, DK * h + DK)
                    for c in reversed(range(NCH)):
                        for kb in range(c // 4 + 1):
                            m = P if kb < c // 4 else CH * (c % 4 + 1)
                            col = CH * c if kb == 0 else T + CH * (c - 4)
                            last = pe.matmul(psum[0:m, h, col:col + CH],
                                             KDEC[rows, CHOFF[c] + kb * P:CHOFF[c] + kb * P + m],
                                             GLQ[rows, CH * c:CH * c + CH], start=True, stop=True)
                last.then_inc(b_scores, 1)
                pe.wait_ge(o_ready, l * 4 + 2)
                qk_scores(DQ, DKEY, GH).then_inc(d_scores, 1)
                pe.wait_ge(pt_ready, l * 4 + 3)
                pe.wait_ge(b_off, l + 1)
                pv(1, 0)
                pe.wait_ge(d_exp, l + 1)
                flip(SD, GH).then_inc(d_flip, 1)
                pe.wait_ge(pt_ready, l * 4 + 4)
                pv(3, 4)
                pe.wait_ge(onrm_ready, l + 1)
                for m in range(4):
                    for k in range(4):
                        last = pe.transpose(psum[:, m, k * P:(k + 1) * P],
                                            ONRM[:, m // 2, (4 * (m % 2) + k) * P:(4 * (m % 2) + k + 1) * P], ident)
                    last.then_inc(ot_done, 1)
                pe.wait_ge(ot_ready, l * 4 + 4)
                for n in range(4):
                    pe.matmul(psum[:, n, :], ident, X[:, n // 2, (n % 2) * 512:(n % 2 + 1) * 512], start=True, stop=False)

                def rows_first(m, ah, al, stop, r=0):
                    ch, cl = card(l, m, r)
                    for n in range(4):
                        tb, half = slice((n // 2) * P, (n // 2 + 1) * P), slice((n % 2) * 512, (n % 2 + 1) * 512)
                        last = product(psum[:, n, :], ah[:, tb], al[:, tb], ch[:, half], cl[:, half], False, stop)
                    last.then_inc(card_used, 1)

                pe.wait_ge(o_low, l + 1)
                for k in range(C_OUT):
                    rows_first(M_OUT + k, HTH[:, k, :], HTL[:, k, :], k == C_OUT - 1)
                pe.wait_ge(x_mixed, l + 1)
                flip_norm(l * 2 + 1)
                pe.wait_ge(h_low, l * 2 + 2)
                for c in range(C_PQ):
                    if c >= 4:
                        pe.wait_ge(pq_read, l * C_PQ + c - 3)
                    columns_first(l, M_PQ + c, c % 4)
                pe.wait_ge(pq_read, l * C_PQ + C_PQ)
                for b in range(NTB):
                    if b:
                        pe.wait_ge(score_read, l * 2 * NTB + 2 * b)
                    for c in range(2 * HEADS):
                        last = pe.matmul(psum[:, 4 + c // 4, (c % 4) * NK:(c % 4 + 1) * NK],
                                         QRY[:, c, b * P:(b + 1) * P], subk[:, c, :], start=True, stop=True)
                        if c % 8 == 7:
                            last.then_inc(score_done, 1)
                pe.wait_ge(score_read, l * 2 * NTB + 2 * NTB)
                def early_columns(r, first):
                    for s in range(4):
                        pe.wait_ge(card_loaded[s], l * (16 * CARDS // SLOTS) + 16 * (M_DENSE // SLOTS) + 16 * r + 16)
                        if s >= 2 or not first:
                            pe.wait_ge(early_read, l * EARLY + r * 4 + s - 1)
                        u = RING[:, s, :].rearrange("p (k i) -> p k i", k=KT)
                        for k in range(KT):
                            last = pe.matmul(psum[:, 4 + s % 2, 0:T], u[:, k, :], HT[:, k, :],
                                             start=(k == 0), stop=(k == KT - 1))
                        last.then_inc(early_done, 1)

                early_columns(0, True)
                with pe.Fori(1, EARLY // 4) as r:
                    early_columns(r, False)
                pe.wait_ge(chosen_ready, l + 1)
                for b in range(NTB):
                    for a in range(3):
                        last = pe.transpose(psum[:, 6 + b, a * P:(a + 1) * P], CHOSEN[:, b, a, :], ident)
                    last.then_inc(route_done, 1)
                for n in range(4):
                    last = pe.matmul(psum[:, n, :], ident, X[:, n // 2, (n % 2) * 512:(n % 2 + 1) * 512],
                                     start=True, stop=False)
                last.then_inc(resid_in, 1)
                pe.wait_ge(route_ready, l + 1)
                pe.wait_ge(start_loaded, 32)
                def gate_groups(r, first):
                    for s in range(4):
                        pe.wait_ge(onehot_ready, l * GROUPS + r * 4 + s + 1)
                        if not first:
                            pe.wait_ge(gate_read, l * GROUPS + r * 4 + s - 3)
                        for t in range(4):
                            last = pe.matmul(psum[:, 4 + s, t * NK:(t + 1) * NK], OH[s][:, 0, t, :], OH[s][:, 1, t, :],
                                             start=True, stop=True)
                        last.then_inc(gate_done, 1)

                gate_groups(0, True)
                with pe.Fori(1, GROUPS // 4) as r:
                    gate_groups(r, False)
                with pe.Fori(0, EARLY // 4) as r:
                    for s in range(4):
                        pe.wait_ge(wt_ready, l * NK + r * 4 + s + 1)
                        rows_first(M_DENSE + s, WH[:, s % 2, :], WL[:, s % 2, :], False, r)
                columns_first(l, M_FIRST, 4)

                def step(r, s, stop):
                    pe.wait_ge(gelu_ready, l * LATE + r * 2 + s)
                    columns_first(l, M_STEP + 2 * s, 4 + (s + 1) % 2, r)
                    pe.wait_ge(wt_ready, l * NK + EARLY + r * 2 + s + 1)
                    rows_first(M_STEP + 1 + 2 * s, WH[:, s % 2, :], WL[:, s % 2, :], stop, r)

                with pe.Fori(0, STEP_PAIRS) as r:
                    for s in range(2):
                        step(r, s, False)
                step(STEP_PAIRS, 0, False)
                pe.wait_ge(wt_ready, (l + 1) * NK)
                rows_first(SPLITS - 1, WH[:, 1, :], WL[:, 1, :], True)


def kernel(x, norm_mix_g, w_in, w_gla_up, b_gla, b_fox, head_norm_g, w_out, norm_ffn_g,
           w_peer_q, peer_sub_keys, peer_u, peer_v, norm_final_g):
    import concourse.bacc as bacc
    from concourse.bass_utils import run_bass_kernel_spmd

    f32 = np.float32
    w_in, w_out, w_peer_q = np.asarray(w_in), np.asarray(w_out), np.asarray(w_peer_q)
    peer_u, peer_v = np.asarray(peer_u), np.asarray(peer_v)

    def columns(w):
        return w.reshape(KT, P, -1, P).transpose(2, 1, 0, 3).reshape(-1, P, CF)

    def halves(w):
        return w.reshape(2, KT // 2, P, -1, 256).transpose(3, 0, 2, 1, 4).reshape(-1, P, CF)

    widths = (256, 256, 256, 128, 128, 256, 256, 16, 256, 256, 256, 256, 256, 256, 4)
    ends = np.cumsum(widths)
    part = [slice(e - w, e) for e, w in zip(ends, widths)]
    by_column, by_token = [0, 1, 3, 4, 8, 9, 11, 12], [2, 5, 10, 13, 6]

    u_at = np.array([M_DENSE + j for j in range(EARLY)] + [M_DENSE + 2 * EARLY]
                    + [M_DENSE + 2 * EARLY + 1 + 2 * n for n in range(LATE - 1)])
    v_at = np.array([M_DENSE + EARLY + j for j in range(EARLY)]
                    + [M_DENSE + 2 * EARLY + 2 + 2 * n for n in range(LATE - 1)] + [CARDS - 1])

    stream = np.empty((DEPTH, CARDS, P, CF), f32)
    sides = np.zeros((DEPTH, P, SIDE_F), f32)
    for l in range(DEPTH):
        stream[l, 0:IN_T] = columns(np.concatenate([w_in[l][:, part[n]] for n in by_column], 1))
        stream[l, IN_T:C_IN] = halves(np.concatenate([w_in[l][:, part[n]] for n in by_token], 1))
        stream[l, M_OUT:M_PQ] = w_out[l].reshape(C_OUT, P, CF)
        stream[l, M_PQ:M_DENSE] = columns(w_peer_q[l])
        stream[l, u_at] = peer_u[l].reshape(P, NK, KT, P).transpose(1, 3, 2, 0).reshape(NK, P, CF)
        stream[l, v_at] = peer_v[l].reshape(P, NK, D).transpose(1, 0, 2)

        def put(name, a):
            s, e = SIDE[name]
            sides[l, :a.shape[0], s:e] = a.reshape(a.shape[0], -1)

        put("subk", np.asarray(peer_sub_keys)[l].transpose(3, 0, 1, 2))
        small = np.zeros((P, KT, SMALL), f32)
        small[:, :, 0:RANK] = w_in[l][:, part[7]].reshape(KT, P, RANK).transpose(1, 0, 2)
        small[:, :, FOX0:] = w_in[l][:, part[14]].reshape(KT, P, GH).transpose(1, 0, 2)
        put("small", small)
        put("up", np.asarray(w_gla_up)[l])
        put("b_gla", np.asarray(b_gla)[l][:, None])
        sides[l, FOX0:SMALL, SIDE["b_fox"][0]] = np.asarray(b_fox)[l]
        put("g_mix", np.asarray(norm_mix_g)[l].reshape(KT, P).T)
        put("g_head", np.asarray(head_norm_g)[l].reshape(KT, P).T)
        put("g_ffn", np.asarray(norm_ffn_g)[l].reshape(KT, P).T)

    mixc, fixed = host_constants()
    arrays = {
        "x_in": np.ascontiguousarray(x),
        "stream": stream.reshape(DEPTH * CARDS, P, CF),
        "side": sides,
        "mixc": mixc,
        "fixed": fixed,
        "gfin": np.ascontiguousarray(np.broadcast_to(np.asarray(norm_final_g), (P, D))),
    }
    nc = bacc.Bacc("TRN2", target_bir_lowering=False, num_devices=1, dynamic_dma_scratch_size=1024)
    aps = [nc.dram_tensor(n, a.shape, F32, kind="ExternalInput").ap() for n, a in arrays.items()]
    y = nc.dram_tensor("y", (1, T, D), F32, kind="ExternalOutput").ap()
    build(nc, *aps, y)
    r = run_bass_kernel_spmd(nc, [arrays], core_ids=[0])
    return r.results[0]["y"]
```

```python
from contextlib import ExitStack

import numpy as np

import concourse.bass as bass
from concourse import mybir

ALU = mybir.AluOpType
ACT = mybir.ActivationFunctionType
AX = mybir.AxisListType
F32 = mybir.dt.float32
BF16 = mybir.dt.bfloat16
F32R = mybir.dt.float32r
U32 = mybir.dt.uint32

P = 128
T = 256
NTB = T // P
D = 1024
KT = D // P
DEPTH = 2
EPS = 1e-6
HD = 64
HV = HD + 1
NH = 16
GH = 4
DK = 32
CH = 32
NCH = T // CH
TAU = 16.0
RANK = 16
FOX0 = 32
SMALL = FOX0 + GH
HEADS = 8
TOPK = 16
NK = 128
HK = HEADS * TOPK
NEG = -1e30
LOWEST = -3.0e38

SLOTS = 4
CF = 1024
C_IN, C_OUT, C_PQ = 24, 8, 16
IN_T = 14
EARLY = 44
LATE = NK - EARLY
M_OUT, M_PQ, M_EARLY = C_IN, C_IN + C_OUT, C_IN + C_OUT + C_PQ
M_DENSE = M_EARLY + EARLY
M_FIRST = M_DENSE
M_STEP = M_FIRST + 1 + EARLY
CARDS = M_EARLY + 2 * NK
SPLITS = CARDS - M_DENSE
assert CARDS % SLOTS == 0 and EARLY % SLOTS == 0 and M_EARLY % SLOTS == 0
AFTER = {"gla_softplus": 3, "a_scores": 4, "gla_decay": 5, "a_tail": 9, "b_scores": 11, "c_scores": 13,
         "fox_gates": 14, "d_scores": 15, "c_flip": 17, "d_flip": 19, "ab_out": 20, "c_out": 22}
STEP_PAIRS = (LATE - 2) // 2

SIDE = {}
_at = 0
for _name, _n in (("subk", 2 * HEADS * NK), ("small", KT * SMALL), ("up", P), ("b_gla", 1), ("b_fox", 1),
                  ("g_mix", KT), ("g_head", KT), ("g_ffn", KT)):
    SIDE[_name] = (_at, _at + _n)
    _at += _n
SIDE_F = _at

MC = {}
_at = 0
for _name, _n in (("tri", P), ("ones", T), ("k_lt_q", P), ("k_le_q", P), ("dil_count", 3 * P),
                  ("dil_bias", GH * 3 * P), ("fox_mask", 3 * P), ("head_sel", GH * P)):
    MC[_name] = (_at, _at + _n)
    _at += _n
MC_F = _at

KQ = 3 * P
CHOFF = [sum(CH * (c + 1) for c in range(n)) for n in range(NCH + 1)]

GROUPS = T // 4


def host_constants():
    p = np.arange(P)[:, None]
    f = np.arange(P)[None, :]
    mc = np.zeros((P, MC_F), np.float32)

    def put(name, a):
        s, e = MC[name]
        mc[:a.shape[0], s:e] = a.reshape(a.shape[0], -1)

    put("tri", (p > f).astype(np.float32))
    put("ones", np.ones((P, T), np.float32))
    put("k_lt_q", (p < f).astype(np.float32))
    put("k_le_q", (p <= f).astype(np.float32))
    d = np.stack([p - f, p - f + P, p - f], 1)
    ok = d >= 0
    count = ok * ((d <= 128).astype(int) + (d % 4 == 0) + (d % 16 == 0))
    put("dil_count", count.astype(np.float32))
    slopes = 2.0 ** (-8.0 * np.arange(1, GH + 1) / GH)
    bias = np.where(count[:, None] > 0, -slopes[None, :, None, None] * d[:, None], NEG)
    put("dil_bias", bias.astype(np.float32))
    put("fox_mask", np.where(ok, 0.0, NEG).astype(np.float32))
    sel = np.zeros((P, GH, P), np.float32)
    for h in range(GH):
        sel[FOX0 + h, h] = 1.0
    put("head_sel", sel)
    fixed = np.concatenate([np.eye(P, dtype=np.float32), np.broadcast_to(f, (P, P)).astype(np.float32)], 1)
    return mc, np.ascontiguousarray(fixed)


def build(nc, x_in, stream, side_in, mixc_in, fixed_in, out):
    with ExitStack() as ctx:
        def sb(name, cols, dt=F32):
            return ctx.enter_context(nc.sbuf_tensor(name, [P, cols], dt))

        def sem(name):
            return ctx.enter_context(nc.semaphore(name))

        X = sb("X", NTB * D)[:].rearrange("p (b d) -> p b d", b=NTB)
        HTH = sb("HTH", KT * T, F32R)[:].rearrange("p (k t) -> p k t", k=KT)
        HTL = sb("HTL", KT * T, F32R)[:].rearrange("p (k t) -> p k t", k=KT)
        REG = sb("REG", NK * T)
        RING = sb("RING", SLOTS * CF)[:].rearrange("p (s c) -> p s c", s=SLOTS)
        CH_ = sb("CARD_HIGH", SLOTS * CF, F32R)[:].rearrange("p (s c) -> p s c", s=SLOTS)
        CL_ = sb("CARD_LOW", SLOTS * CF, F32R)[:].rearrange("p (s c) -> p s c", s=SLOTS)
        WH = sb("WH", 2 * T, F32R)[:].rearrange("p (b t) -> p b t", b=2)
        WL = sb("WL", 2 * T, F32R)[:].rearrange("p (b t) -> p b t", b=2)
        SIDEB = sb("SIDEB", SIDE_F)
        FIX = sb("FIX", 2 * P)
        ROUTE = sb("ROUTE", 2 * T, BF16)[:].rearrange("p (a t) -> p a t", a=2)
        GATE = sb("GATE", T)
        IOTA4 = sb("IOTA4", 4 * NK, BF16)[:].rearrange("p (n t) -> p n t", t=4)
        OHB = [sb(f"OHB{n}", 8 * NK, BF16)[:].rearrange("p (a n t) -> p a n t", a=2, t=4) for n in range(2)]
        TINY = sb("TINY", 260)
        psum = ctx.enter_context(nc.psum_tensor("psum", [P, 8, 512], F32))

        ident = FIX[:, 0:P]
        iota = FIX[:, P:2 * P]

        def side(name):
            s, e = SIDE[name]
            return SIDEB[:, s:e]

        subk = side("subk").rearrange("p (c n) -> p c n", n=NK)
        wsmall = side("small").rearrange("p (k c) -> p k c", k=KT)

        at = [0]

        top = [NK * T - 2 * KT * T]

        def reg(n):
            at[0] += n
            assert at[0] <= top[0]
            return REG[:, at[0] - n:at[0]]

        mixc = reg(MC_F)

        def mc(name):
            s, e = MC[name]
            return mixc[:, s:e]

        XN = REG[:, NK * T - NTB * D:].rearrange("p (b d) -> p b d", b=NTB)
        HT = REG[:, NK * T - 2 * NTB * D:NK * T - NTB * D].rearrange("p (k t) -> p k t", k=KT)
        DIAG = XN[:, 0, 0:T].rearrange("p (b t) -> p b t", b=NTB)
        ONES, SPREAD = XN[:, 0, T:T + P], XN[:, 1, 0:T]
        GFIN = SIDEB[:, 0:D]
        QK = reg(14 * T).rearrange("p (c t) -> p c t", t=T)
        AQ, AK, BQ, BK, CQ, CK, DQ, DKEY = 0, 2, 4, 5, 6, 8, 10, 12
        VN = reg(NTB * NH * HV).rearrange("p (b h v) -> p b h v", b=NTB, h=NH)
        RN = reg(NTB * T).rearrange("p (b c) -> p b c", b=NTB)
        SIG = reg(NTB * T).rearrange("p (b c) -> p b c", b=NTB)
        GDT = reg(T)
        GLY, GLA_A, GLC, GLQ = reg(T), reg(T), reg(T), reg(T)
        FOXY, FOXA, FOXC = reg(T), reg(T), reg(T)
        KDEC = reg(CHOFF[NCH])
        PT = [reg(GH * KQ).rearrange("p (h c) -> p h c", h=GH) for _ in range(4)]
        scores_at = at[0]
        SA, SB_, SC, SD = [reg(GH * KQ).rearrange("p (h c) -> p h c", h=GH) for _ in range(4)]
        OALL = reg(NTB * NH * HV)
        GLQD = OALL[:, 0:GH * T].rearrange("p (n h q) -> p n h q", n=NCH, h=GH)
        OALL = OALL.rearrange("p (b h v) -> p b h v", b=NTB, h=NH)
        OSQ = REG[:, scores_at:scores_at + NTB * D].rearrange("p (b h v) -> p b h v", b=NTB, h=NH)
        OT = REG[:, scores_at + 2 * GH * KQ:scores_at + 2 * GH * KQ + KT * T].rearrange("p (k t) -> p k t", k=KT)
        ONRM = XN

        at[0], top[0] = EARLY * T, NK * T
        QRY = reg(2 * HEADS * T).rearrange("p (c t) -> p c t", t=T)
        SCO = reg(NTB * 2 * HEADS * NK).rearrange("p (b c n) -> p b c n", b=NTB, n=NK)
        SCO2 = reg(2 * HEADS * NK).rearrange("p (c n) -> p c n", n=NK)
        CAND = reg(HEADS * 256).rearrange("p (h n) -> p h n", h=HEADS)
        CAND2 = reg(HEADS * 256).rearrange("p (h n) -> p h n", h=HEADS)
        PICK = reg(HEADS * 256).rearrange("p (h k a) -> p h k a", h=HEADS, k=TOPK)
        PICK2 = reg(HEADS * 256).rearrange("p (h k a) -> p h k a", h=HEADS, k=TOPK)
        TOPV = reg(2 * HK).rearrange("p (c k) -> p c k", k=TOPK)
        TOPI = reg(2 * HK).bitcast(U32).rearrange("p (c k) -> p c k", k=TOPK)
        TOPF = reg(2 * HK).rearrange("p (h c k) -> p h c k", c=2, k=TOPK)
        BEST = reg(HK).rearrange("p (h k) -> p h k", k=TOPK)
        POS = reg(HK).bitcast(U32).rearrange("p (h k) -> p h k", k=TOPK)
        POSA = reg(2 * HK).bitcast(U32).rearrange("p (c h k) -> p c h k", c=2, k=TOPK)
        POSF = reg(2 * HK).rearrange("p (c h k) -> p c h k", c=2, k=TOPK)
        CHOSEN = reg(NTB * 3 * HK).rearrange("p (b a c) -> p b a c", b=NTB, a=3)
        GSH = reg(NTB * HK).rearrange("p (b h k) -> p b h k", b=NTB, k=TOPK)
        G = REG[:, :].rearrange("p (j t) -> p j t", t=T)

        XF = X.rearrange("p b d -> p (b d)")
        OH = [t.rearrange("p (a t n) -> p a t n", a=2, t=4)
              for t in (XF[:, 0:D], XF[:, D:], SIDEB[:, 0:D], SIDEB[:, D:2 * D])]
        GEL = XF[:, 0:2 * T].rearrange("p (b t) -> p b t", b=2)

        SUMSQ, VAR, RT1 = TINY[:, 0:4], TINY[:, 4:6], TINY[:, 8:10]
        RSTD = TINY[:, 10:12]
        NRMID = TINY[:, 16:16 + NCH]
        MAXN = TINY[:, 32:48].rearrange("p (g b h) -> p g b h", g=2, b=NTB)
        RDEN = TINY[:, 48:64].rearrange("p (b h) -> p b h", b=NTB)
        HSS, HVAR, HTMP, HRS = [TINY[:, 64 + 32 * n:96 + 32 * n] for n in range(4)]
        GSUM = TINY[:, 224:240].rearrange("p (b h) -> p b h", b=NTB)
        GREC = TINY[:, 240:256].rearrange("p (b h) -> p b h", b=NTB)

        card_loaded = [sem(f"card_loaded{n}") for n in range(SLOTS)]
        high_ready = sem("high_ready")
        split_ready = sem("split_ready")
        card_used = sem("card_used")
        early_read = sem("early_read")
        h_high = sem("h_high")
        h_low = sem("h_low")
        o_low = sem("o_low")
        o_high = sem("o_high")
        resid_in = sem("resid_in")
        start_loaded = sem("start_loaded")
        side_loaded = sem("side_loaded")
        mixc_loaded = sem("mixc_loaded")
        x_sum = sem("x_sum")
        squared = sem("squared")
        x_taken = sem("x_taken")
        x_last = sem("x_last")
        diag_ready = sem("diag_ready")
        rstd_spread = sem("rstd_spread")
        xt_done = sem("xt_done")
        ht_ready = sem("ht_ready")
        small_done = sem("small_done")
        gd_ready = sem("gd_ready")
        gl_done = sem("gl_done")
        gly_ready = sem("gly_ready")
        gls_ready = sem("gls_ready")
        glc_ready = sem("glc_ready")
        gle_ready = sem("gle_ready")
        glq_ready = sem("glq_ready")
        foxy_ready = sem("foxy_ready")
        foxs_ready = sem("foxs_ready")
        foxc_ready = sem("foxc_ready")
        foxb_done = sem("foxb_done")
        foxb_read = sem("foxb_read")
        proj_read = sem("proj_read")
        r_exp = sem("r_exp")
        a_scores = sem("a_scores")
        a_soft = sem("a_soft")
        a_sp = sem("a_sp")
        a_tail = sem("a_tail")
        a_logw = sem("a_logw")
        a_exp = sem("a_exp")
        b_zeroed = sem("b_zeroed")
        b_scores = sem("b_scores")
        b_off = sem("b_off")
        c_scores = sem("c_scores")
        c_read = sem("c_read")
        c_logits = sem("c_logits")
        c_exp = sem("c_exp")
        c_prob = sem("c_prob")
        c_flip = sem("c_flip")
        d_scores = sem("d_scores")
        d_read = sem("d_read")
        d_logits = sem("d_logits")
        d_exp = sem("d_exp")
        d_flip = sem("d_flip")
        a_ready = sem("a_ready")
        b_ready = sem("b_ready")
        c_ready = sem("c_ready")
        d_ready = sem("d_ready")
        pv_done = sem("pv_done")
        o_ready = sem("o_ready")
        o_scaled = sem("o_scaled")
        o_sq = sem("o_sq")
        onrm_ready = sem("onrm_ready")
        ot_done = sem("ot_done")
        ot_ready = sem("ot_ready")
        pq_read = sem("pq_read")
        score_done = sem("score_done")
        score_read = sem("score_read")
        gate_shift = sem("gate_shift")
        gate_exp = sem("gate_exp")
        chosen_ready = sem("chosen_ready")
        route_done = sem("route_done")
        route_ready = sem("route_ready")
        onehot_equal = sem("onehot_equal")
        onehot_i = sem("onehot_i")
        onehot_j = sem("onehot_j")
        pool_split = sem("pool_split")
        gate_copied = sem("gate_copied")
        gate_done = sem("gate_done")
        gate_read = sem("gate_read")
        gelu_ready = sem("gelu_ready")
        wt_ready = sem("wt_ready")
        x_loaded = sem("x_loaded")
        y_ready = sem("y_ready")
        stored = sem("stored")

        block = ctx.enter_context(nc.Block())

        def v_bank(p):
            return 4 + 2 * ((p + 1) % 2)

        def by_batch(t, q):
            return t.rearrange("p (b h) -> p b h", b=NTB)[:, :, 8 * q:8 * q + 8]

        @block.sync
        def _(sp):
            def load(l, first, r, slot):
                sp.dma_start(RING[:, slot, :], stream[l * CARDS + first + r * SLOTS + slot])\
                    .then_inc(card_loaded[slot], 16)

            with sp.Fori(0, DEPTH) as l:
                for slot in range(SLOTS):
                    sp.wait_ge(split_ready, l * SPLITS + slot + 1)
                    sp.dma_start(RING[:, slot, :], stream[l * CARDS + slot]).then_inc(card_loaded[slot], 16)
                with sp.Fori(0, M_DENSE // SLOTS) as r:
                    for slot in range(SLOTS):
                        sp.wait_ge(pool_split, l * M_DENSE + r * SLOTS + slot + 1)
                        load(l, SLOTS, r, slot)
                with sp.Fori(0, (CARDS - M_DENSE - SLOTS) // SLOTS) as r:
                    for slot in range(SLOTS):
                        sp.wait_ge(split_ready, l * SPLITS + SLOTS + r * SLOTS + slot + 1)
                        load(l, M_DENSE + SLOTS, r, slot)
            for b in range(NTB):
                sp.wait_ge(y_ready, b + 1)
                sp.dma_start(out[0, b * P:(b + 1) * P, :], XN[:, b, :]).then_inc(stored, 16)
            sp.wait_ge(stored, NTB * 16)

        @block.gpsimd
        def _(pool):
            with pool.Fori(0, DEPTH) as l:
                with pool.Fori(0, M_DENSE // SLOTS) as r:
                    for s in range(SLOTS):
                        pool.wait_ge(high_ready, l * CARDS + r * SLOTS + s + 1)
                        pool.tensor_tensor(CL_[:, s, :], RING[:, s, :], CH_[:, s, :].bitcast(F32),
                                           ALU.subtract).then_inc(pool_split, 1)
                def onehot_i_rows(r, first):
                    for s in range(4):
                        if not first:
                            pool.wait_ge(gate_done, l * GROUPS + r * 4 + s - 3)
                        pool.wait_ge(onehot_equal, l * GROUPS + r * 4 + s + 1)
                        gates = GATE[:, bass.ds(r * 16 + s * 4, 4)].unsqueeze(2).to_broadcast([P, 4, NK])
                        pool.tensor_tensor(OH[s][:, 0], OHB[s % 2][:, 0].rearrange("p n t -> p t n"), gates,
                                           ALU.mult).then_inc(onehot_i, 1)

                onehot_i_rows(0, True)
                with pool.Fori(1, GROUPS // 4) as r:
                    onehot_i_rows(r, False)

        @block.scalar
        def _(act):
            def x_chunk(t, n):
                return t[:, n // 2, (n % 2) * 512:(n % 2 + 1) * 512]

            def square(src, n):
                act.activation(x_chunk(XN, n), src, ACT.Square, scale=D ** -0.5,
                               accum_out=SUMSQ[:, n:n + 1]).then_inc(squared, 1)

            def square_sums(norm, last_card):
                for n in range(4):
                    if n < 3:
                        act.wait_ge(x_sum, norm * 3 - 3 + n + 1)
                    else:
                        act.wait_ge(card_used, last_card)
                    square(psum[:, n, :], n)
                act.copy(x_chunk(X, 3), psum[:, 3, :]).then_inc(x_last, 1)

            def norm_high(norm):
                for k in range(0, KT, 2):
                    act.wait_ge(ht_ready, norm * KT + k + 2)
                    act.copy(HTH[:, k:k + 2, :], HT[:, k:k + 2, :]).then_inc(h_high, 1)

            def head_square(l, q):
                if q == 0:
                    act.wait_ge(o_ready, l * 4 + 2)
                else:
                    act.wait_ge(o_scaled, l + 1)
                act.activation(OSQ[:, :, 8 * q:8 * q + 8, :], OALL[:, :, 8 * q:8 * q + 8, 0:HD],
                               ACT.Square).then_inc(o_sq, 1)

            def heads_high(l, q):
                act.wait_ge(ot_ready, l * 4 + 2 * q + 2)
                act.copy(HTH[:, 4 * q:4 * q + 4, :], OT[:, 4 * q:4 * q + 4, :]).then_inc(o_high, 1)

            def softplus_exp(pairs):
                for dst, src in pairs:
                    act.activation(dst, src, ACT.Abs)
                act.drain()
                for dst, src in pairs:
                    act.activation(dst, dst, ACT.Exp, scale=-1.0)
                act.drain()

            def softplus_log(dst):
                return act.activation(dst, dst, ACT.Ln, bias=1.0)

            def softmax_exp(t, g):
                for b in range(NTB):
                    for h in range(GH):
                        cols = slice(0, P) if b == 0 else slice(P, KQ)
                        last = act.activation(t[:, h, cols], t[:, h, cols], ACT.Exp, bias=MAXN[:, g, b, h:h + 1])
                return last

            def high(l, m, r=0):
                act.wait_ge(card_loaded[m % SLOTS], l * (16 * CARDS // SLOTS) + 16 * (m // SLOTS) + 16 * r + 16)
                if m >= SLOTS:
                    act.wait_ge(card_used, l * CARDS + m - SLOTS + 1 + SLOTS * r)
                act.copy(CH_[:, m % SLOTS, :], RING[:, m % SLOTS, :]).then_inc(high_ready, 1)

            act.dma_start(X, x_in.rearrange("a (b p) d -> p (a b) d", p=P)).then_inc(x_loaded, 16)
            act.dma_start(FIX[:, :], fixed_in).then_inc(start_loaded, 16)
            act.dma_start(SIDEB[:, :], side_in[0]).then_inc(side_loaded, 16)
            act.wait_ge(x_loaded, 16)
            for n in range(4):
                square(x_chunk(X, n), n)
            act.dma_start(mixc, mixc_in).then_inc(mixc_loaded, 16)
            with act.Fori(0, DEPTH) as l:
                for m in range(3):
                    high(l, m)
                norm_high(l * 2)
                act.wait_ge(small_done, l + 1)
                act.copy(GDT[0:RANK, :], psum[0:RANK, 0, 0:T]).then_inc(gd_ready, 1)
                for c in range(C_IN):
                    high(l, c + 3)
                    if c == AFTER["gla_softplus"] + 1:
                        act.wait_ge(foxy_ready, l + 1)
                        act.wait_ge(gly_ready, l + 1)
                        softplus_exp([(GLA_A, GLY), (FOXA[FOX0:SMALL, :], FOXY[FOX0:SMALL, :])])
                        softplus_log(GLA_A).then_inc(gls_ready, 1)
                        softplus_log(FOXA[FOX0:SMALL, :]).then_inc(foxs_ready, 1)
                    if c == AFTER["a_scores"] + 1:
                        act.wait_ge(a_scores, l + 1)
                        softplus_exp([(SA[:, :, :], psum[:, 0:GH, 0:KQ])])
                        softplus_log(SA[:, :, :]).then_inc(a_soft, 1)
                    if c == AFTER["gla_decay"] + 1:
                        act.wait_ge(glc_ready, l + 1)
                        for n in range(NCH):
                            act.activation(KDEC[:, CHOFF[n]:CHOFF[n + 1]], GLC[:, 0:CH * (n + 1)], ACT.Exp,
                                           bias=NRMID[:, n:n + 1], scale=1.0 / TAU)
                        act.activation(GLQ, GLQ, ACT.Exp, scale=-1.0 / TAU).then_inc(gle_ready, 1)
                    if c == AFTER["a_tail"] + 2:
                        act.wait_ge(a_logw, l + 1)
                        act.activation(PT[0][:, :, :], SA[:, :, :], ACT.Exp).then_inc(a_exp, 1)
                    if c == AFTER["b_scores"] + 1:
                        act.wait_ge(b_scores, l + 1)
                        act.copy(PT[1][:, :, P:2 * P].rearrange("p h (n q) -> p h n q", q=CH),
                                 psum[:, 1, :].rearrange("p (n h q) -> p h n q", h=GH, q=CH)).then_inc(b_off, 1)
                    if c == AFTER["c_scores"] + 2:
                        act.wait_ge(c_logits, l + 1)
                        softmax_exp(SC, 0).then_inc(c_exp, 1)
                    if c == AFTER["d_scores"] + 2:
                        act.wait_ge(d_logits, l + 1)
                        softmax_exp(SD, 1).then_inc(d_exp, 1)
                    if c == AFTER["c_flip"] + 1:
                        act.wait_ge(c_flip, l + 1)
                        act.copy(PT[2][:, :, :], psum[:, 0:GH, 0:KQ]).then_inc(c_ready, 1)
                    if c == AFTER["d_flip"] + 1:
                        act.wait_ge(d_flip, l + 1)
                        act.copy(PT[3][:, :, :], psum[:, 0:GH, 0:KQ]).then_inc(d_ready, 1)
                    if c == AFTER["ab_out"] + 1:
                        head_square(l, 0)
                    act.wait_ge(card_used, l * CARDS + c + 1)
                    if c < IN_T:
                        act.activation(QK[:, c, :], psum[:, 4 + c % 4, 0:T], ACT.Copy,
                                       scale=0.125 if c in (0, 1, 6, 7, 10, 11) else 1.0).then_inc(proj_read, 1)
                    elif c % 2:
                        if c == IN_T + 3:
                            act.wait_ge(b_zeroed, l + 1)
                        p = (c - IN_T) // 2
                        for b in range(NTB):
                            src = psum[:, v_bank(p) + b, 0:T]
                            if p == 0:
                                last = act.copy(RN[:, b, :], src)
                            else:
                                last = act.copy(VN[:, b, GH * p - GH:GH * p, 0:HD],
                                                src.rearrange("p (h v) -> p h v", h=GH))
                        last.then_inc(proj_read, 1)
                    if c == IN_T + 1:
                        act.drain()
                        act.activation(SIG[:, :, :], RN[:, :, :], ACT.Exp, scale=-1.0).then_inc(r_exp, 1)
                heads_high(l, 0)
                head_square(l, 1)
                for u in range(3):
                    high(l, M_OUT + u + 3)
                heads_high(l, 1)
                for u in range(3, C_OUT):
                    high(l, M_OUT + u + 3)
                square_sums(l * 2 + 1, l * CARDS + M_PQ)
                norm_high(l * 2 + 1)
                for c in range(C_PQ):
                    high(l, M_PQ + c + 3)
                    act.wait_ge(card_used, l * CARDS + M_PQ + c + 1)
                    act.copy(QRY[:, c, :], psum[:, 4 + c % 4, 0:T]).then_inc(pq_read, 1)
                for b in range(NTB):
                    for n in range(2):
                        act.wait_ge(score_done, l * 2 * NTB + 2 * b + n + 1)
                        act.copy(SCO[:, b, 8 * n:8 * n + 8, :], psum[:, 4 + 2 * n:6 + 2 * n, :]
                                 .rearrange("p b (c n) -> p (b c) n", n=NK)).then_inc(score_read, 1)
                def early_gelu(r, s):
                    high(l, M_EARLY + 3 + s, r)
                    act.wait_ge(card_used, l * CARDS + M_EARLY + r * 4 + s + 1)
                    act.activation(G[:, bass.ds(r * 4 + s, 1), :], psum[:, 4 + s % 2, 0:T].unsqueeze(1),
                                   ACT.Gelu).then_inc(early_read, 1)

                with act.Fori(0, EARLY // 4 - 1) as r:
                    for s in range(4):
                        early_gelu(r, s)
                for s in range(4):
                    if s == 0:
                        act.wait_ge(gate_shift, l + 1)
                        act.activation(GSH[:, :, :, :], GSH[:, :, :, :], ACT.Exp).then_inc(gate_exp, 1)
                    early_gelu(EARLY // 4 - 1, s)
                def onehot_j_rows(r, s):
                    act.wait_ge(onehot_equal, l * GROUPS + r * 4 + s + 1)
                    act.copy(OH[s % 4][:, 1], OHB[s % 2][:, 1].rearrange("p n t -> p t n")).then_inc(onehot_j, 1)

                def late_gates(r, s):
                    act.wait_ge(gate_done, l * GROUPS + r * 4 + s + 1)
                    act.copy(G[:, EARLY:, bass.ds(r * 16 + s * 4, 4)],
                             psum[:, 4 + s, :].rearrange("p (t j) -> p j t", t=4)[:, EARLY:, :])\
                        .then_inc(gate_copied, 1)

                for s in range(3):
                    onehot_j_rows(0, s)
                with act.Fori(0, GROUPS // 4 - 1) as r:
                    for s in range(4):
                        late_gates(r, s)
                        onehot_j_rows(r, s + 3)
                for s in range(4):
                    late_gates(GROUPS // 4 - 1, s)
                    if s < 1:
                        onehot_j_rows(GROUPS // 4 - 1, s + 3)
                act.dma_start(SIDEB[:, :], side_in[l + 1]).then_inc(side_loaded, 16)
                with act.Fori(0, EARLY // 4) as r:
                    for s in range(4):
                        high(l, M_DENSE + 3 + s, r)

                def gelu_late(n, used, a):
                    act.wait_ge(card_used, l * CARDS + used)
                    act.wait_ge(wt_ready, l * NK + EARLY + n - 1)
                    act.activation(GEL[:, a, :], psum[:, 4 + a, 0:T], ACT.Gelu).then_inc(gelu_ready, 1)

                gelu_late(0, M_FIRST + 1, 0)
                act.dma_start(mixc, mixc_in).then_inc(mixc_loaded, 16)
                with act.Fori(0, STEP_PAIRS) as r:
                    for s in range(2):
                        high(l, M_STEP + 2 + 2 * s, r)
                        high(l, M_STEP + 3 + 2 * s, r)
                        gelu_late(r * 2 + s + 1, M_STEP + 1 + 2 * s + r * 4, (s + 1) % 2)
                high(l, CARDS - 1)
                gelu_late(LATE - 1, CARDS - 2, 1)
                square_sums(l * 2 + 2, l * CARDS + CARDS)
            act.wait_ge(mixc_loaded, DEPTH * 16 + 16)

        @block.vector
        def _(dve):
            def rsqrt(dst, tmp, src):
                dve.tensor_scalar(dst.bitcast(U32), src.bitcast(U32), 1, None, ALU.logical_shift_right)
                dve.drain()
                dve.tensor_scalar(dst.bitcast(U32), dst.bitcast(U32), -1.0, float(0x5f3759df), ALU.mult, ALU.add)
                dve.drain()
                for _ in range(3):
                    dve.tensor_tensor(tmp, dst, dst, ALU.mult)
                    dve.drain()
                    dve.scalar_tensor_tensor(tmp, tmp, -0.5, src, ALU.mult, ALU.mult)
                    dve.drain()
                    dve.scalar_tensor_tensor(dst, tmp, 1.5, dst, ALU.add, ALU.mult)
                    dve.drain()

            def norm_rstd(norm):
                dve.wait_ge(squared, norm * 4 + 4)
                dve.scalar_tensor_tensor(VAR, SUMSQ[:, 0:4:2], EPS, SUMSQ[:, 1:4:2], ALU.add, ALU.add)
                dve.drain()
                rsqrt(RSTD, RT1, VAR)

            def take_x(norm):
                for n in range(3):
                    dve.wait_ge(squared, norm * 4 + n + 1)
                    dve.tensor_copy(X[:, n // 2, (n % 2) * 512:(n % 2 + 1) * 512], psum[:, n, :])\
                        .then_inc(x_taken, 1)

            def low(l, m, r=0):
                dve.wait_ge(high_ready, l * CARDS + m + 1 + SLOTS * r)
                dve.tensor_tensor(CL_[:, m % SLOTS, :], RING[:, m % SLOTS, :], CH_[:, m % SLOTS, :].bitcast(F32),
                                  ALU.subtract).then_inc(split_ready, 1)

            def norm(n, gain, side_count=None):
                norm_rstd(n)
                dve.memset(ONES, 1.0)
                for b in range(NTB):
                    last = dve.tensor_scalar(DIAG[:, b, :], ident, RSTD[:, b:b + 1], None, ALU.mult)
                last.then_inc(diag_ready, 1)
                if side_count is not None:
                    dve.wait_ge(side_loaded, side_count)
                dve.wait_ge(rstd_spread, n + 1)
                dve.tensor_copy(SPREAD, psum[:, 3, 0:T])
                dve.drain()
                spread = SPREAD.rearrange("p (b t) -> p b t", b=NTB)
                for q in range(2):
                    dve.wait_ge(xt_done, n * 4 + 2 * q + 2)
                    for k in range(4 * q, 4 * q + 4):
                        kk = slice((k % 4) * P, (k % 4 + 1) * P)
                        dve.scalar_tensor_tensor(HT[:, k, :].rearrange("p (b t) -> p b t", b=NTB),
                                                 psum[:, 4 + 2 * q:6 + 2 * q, kk], gain[:, k:k + 1], spread,
                                                 ALU.mult, ALU.mult).then_inc(ht_ready, 1)
                    for k in (4 * q, 4 * q + 2):
                        dve.wait_ge(h_high, n * 4 + k // 2 + 1)
                        dve.tensor_tensor(HTL[:, k:k + 2, :], HT[:, k:k + 2, :], HTH[:, k:k + 2, :].bitcast(F32),
                                          ALU.subtract).then_inc(h_low, 1)

            def head_norm(l, q):
                dve.wait_ge(o_sq, l * 2 + q + 1)
                dve.tensor_reduce(by_batch(HSS, q), OSQ[:, :, 8 * q:8 * q + 8, :], AX.X, ALU.add)
                dve.drain()
                dve.tensor_scalar(by_batch(HVAR, q), by_batch(HSS, q), 1.0 / HD, EPS, ALU.mult, ALU.add)
                dve.drain()
                rsqrt(by_batch(HRS, q), by_batch(HTMP, q), by_batch(HVAR, q))
                onrm = ONRM.rearrange("p b (h v) -> p b h v", h=NH)[:, :, 8 * q:8 * q + 8, :]
                return dve.tensor_tensor(onrm, OALL[:, :, 8 * q:8 * q + 8, 0:HD],
                                         by_batch(HRS, q).unsqueeze(3).to_broadcast([P, NTB, 8, HD]), ALU.mult)

            def heads_transposed(l, q, bank):
                for b in range(NTB):
                    dve.wait_ge(ot_done, l * 4 + 2 * q + b + 1)
                    dve.tensor_tensor(OT[:, 4 * q:4 * q + 4, b * P:(b + 1) * P],
                                      psum[:, bank + b, :].rearrange("p (k t) -> p k t", k=4),
                                      side("g_head")[:, 4 * q:4 * q + 4].unsqueeze(2).to_broadcast([P, 4, P]),
                                      ALU.mult).then_inc(ot_ready, 1)

            def heads_low(l, q):
                dve.wait_ge(o_high, l * 2 + q + 1)
                half = slice(4 * q, 4 * q + 4)
                dve.tensor_tensor(HTL[:, half, :], OT[:, half, :], HTH[:, half, :].bitcast(F32),
                                  ALU.subtract).then_inc(o_low, 1)

            def diagonal(t):
                return t.rearrange("p h (b q) -> p h b q", b=3)[:, :, 0:3:2, :]

            def masked(t, src, name):
                m = mc(name).unsqueeze(1).to_broadcast([P, 2, P]).unsqueeze(1).to_broadcast([P, GH, 2, P])
                return dve.tensor_tensor(diagonal(t), diagonal(src), m, ALU.mult)

            def row_max(src, g):
                dve.tensor_reduce(MAXN[:, g, 0, :], src[:, :, 0:P], AX.X, ALU.max)
                dve.tensor_reduce(MAXN[:, g, 1, :], src[:, :, P:KQ], AX.X, ALU.max)
                dve.drain()
                return dve.tensor_scalar(MAXN[:, g, :, :], MAXN[:, g, :, :], -1.0, None, ALU.mult)

            def take_o(l, g, bank, order):
                dve.wait_ge(pv_done, l * 4 + order)
                for b in range(NTB):
                    last = dve.tensor_copy(OALL[:, b, GH * g:GH * g + GH, :],
                                           psum[:, bank + b, 0:GH * HV].rearrange("p (h v) -> p h v", h=GH))
                last.then_inc(o_ready, 1)

            dve.memset(TINY[:, 256:260], 0.0).then_inc(split_ready, SLOTS)
            dve.memset(TINY[:, 24:28], 0.0).then_inc(x_taken, 3)
            dve.memset(TINY[:, 12:16], 0.0).then_inc(x_last, 1)
            dve.wait_ge(start_loaded, 16)
            dve.tensor_copy(IOTA4, iota.unsqueeze(2).to_broadcast([P, NK, 4]))
            with dve.Fori(0, DEPTH) as l:
                norm(l * 2, side("g_mix"), l * 16 + 16)
                dve.wait_ge(mixc_loaded, l * 16 + 16)
                dve.wait_ge(small_done, l + 1)
                dve.tensor_scalar(FOXY[FOX0:SMALL, :], psum[FOX0:SMALL, 0, 0:T],
                                  side("b_fox")[FOX0:SMALL, :], -1.0, ALU.add, ALU.mult).then_inc(foxy_ready, 1)
                dve.wait_ge(gl_done, l + 1)
                dve.tensor_scalar(GLY, psum[:, 1, 0:T], side("b_gla"), -1.0, ALU.add, ALU.mult).then_inc(gly_ready, 1)
                dve.memset(PT[1][:, :, :], 0.0)
                dve.memset(GLQD, 0.0)
                dve.memset(VN[:, :, :, HD:HV], 1.0).then_inc(b_zeroed, 1)
                dve.wait_ge(gls_ready, l + 1)
                dve.scalar_tensor_tensor(GLA_A, GLY, 0.0, GLA_A, ALU.max, ALU.add)
                dve.drain()
                dve.tensor_tensor_scan(GLC, mc("ones"), GLA_A, 0.0, ALU.mult, ALU.add)
                dve.drain()
                mid = GLC.rearrange("p (c s) -> p c s", s=CH)[:, :, CH // 2 - 1:CH // 2]
                dve.tensor_scalar(NRMID.unsqueeze(2), mid, -1.0 / TAU, None, ALU.mult)
                dve.tensor_tensor(GLQ.rearrange("p (c s) -> p c s", s=CH), GLC.rearrange("p (c s) -> p c s", s=CH),
                                  mid.to_broadcast([P, NCH, CH]), ALU.subtract).then_inc(glc_ready, 1)
                dve.wait_ge(foxs_ready, l + 1)
                rows = slice(FOX0, SMALL)
                dve.scalar_tensor_tensor(FOXA[rows, :], FOXY[rows, :], 0.0, FOXA[rows, :], ALU.max, ALU.add)
                dve.drain()
                dve.tensor_tensor_scan(FOXC[rows, :], mc("ones")[rows, :], FOXA[rows, :], 0.0,
                                       ALU.mult, ALU.add).then_inc(foxc_ready, 1)
                dve.wait_ge(a_soft, l + 1)
                dve.scalar_tensor_tensor(SA[:, :, :], psum[:, 0:GH, 0:KQ], 0.0, SA[:, :, :], ALU.max, ALU.add)
                dve.drain()
                dve.tensor_tensor(SB_[:, :, :], psum[:, 0:GH, 0:KQ], SA[:, :, :], ALU.subtract)
                dve.drain()
                masked(SA, SA, "k_lt_q").then_inc(a_sp, 1)
                dve.wait_ge(gle_ready, l + 1)
                dve.wait_ge(proj_read, l * (IN_T + 5) + 6)
                for h in range(GH):
                    rows = slice(DK * h, DK * h + DK)
                    dve.scalar_tensor_tensor(GLQD[rows, :, h, :],
                                             GLQ[rows, :].rearrange("p (n q) -> p n q", q=CH), DK ** -0.5,
                                             QK[rows, BQ, :].rearrange("p (n q) -> p n q", q=CH), ALU.mult, ALU.mult)
                for c in range(NCH):
                    last = dve.tensor_tensor(KDEC[:, CHOFF[c]:CHOFF[c + 1]], KDEC[:, CHOFF[c]:CHOFF[c + 1]],
                                             QK[:, BK, 0:CH * (c + 1)], ALU.mult)
                last.then_inc(glq_ready, 1)
                dve.wait_ge(a_tail, l + 1)
                dve.tensor_tensor(SA[:, :, :], SB_[:, :, :], psum[:, 0:GH, 0:KQ], ALU.subtract).then_inc(a_logw, 1)
                dve.wait_ge(b_off, l + 1)
                for m in range(4):
                    r = CH * (m + 1)
                    cols = slice(CH * m, CH * m + CH)
                    mask = mc("k_le_q")[0:r, cols].unsqueeze(1).to_broadcast([r, GH, CH]).unsqueeze(1)\
                        .to_broadcast([r, 2, GH, CH])
                    last = dve.tensor_tensor(diagonal(PT[1])[0:r, :, :, cols].rearrange("p h b q -> p b h q"),
                                             psum[0:r, 0:3:2, P * m:P * m + P].rearrange("p b (h q) -> p b h q", q=CH),
                                             mask, ALU.mult)
                last.then_inc(b_ready, 1)
                dve.wait_ge(a_exp, l + 1)
                masked(PT[0], PT[0], "k_lt_q").then_inc(a_ready, 1)
                dve.wait_ge(c_scores, l + 1)
                dve.tensor_tensor(SC[:, :, :], psum[:, 0:GH, 0:KQ],
                                  mc("dil_bias").rearrange("p (h c) -> p h c", h=GH), ALU.add).then_inc(c_read, 1)
                dve.drain()
                row_max(SC, 0).then_inc(c_logits, 1)
                dve.wait_ge(foxb_done, l + 1)
                for h in range(GH):
                    fb = psum[:, h, :]
                    dve.tensor_tensor(SD[:, h, 0:P], fb[:, 0:P], mc("fox_mask")[:, 0:P], ALU.add)
                    last = dve.tensor_tensor(SD[:, h, P:KQ], fb[:, 0:T], mc("fox_mask")[:, P:KQ], ALU.add)
                last.then_inc(foxb_read, 1)
                dve.wait_ge(d_scores, l + 1)
                dve.tensor_tensor(SD[:, :, :], psum[:, 0:GH, 0:KQ], SD[:, :, :], ALU.add).then_inc(d_read, 1)
                dve.wait_ge(c_exp, l + 1)
                dve.tensor_tensor(SC[:, :, :], SC[:, :, :],
                                  mc("dil_count").unsqueeze(1).to_broadcast([P, GH, KQ]), ALU.mult).then_inc(c_prob, 1)
                dve.drain()
                row_max(SD, 1).then_inc(d_logits, 1)
                dve.wait_ge(r_exp, l + 1)
                dve.tensor_scalar(SIG[:, :, :], SIG[:, :, :], 1.0, None, ALU.add)
                dve.drain()
                dve.reciprocal(SIG[:, :, :], SIG[:, :, :])
                dve.drain()
                dve.tensor_tensor(SIG[:, :, :], SIG[:, :, :], RN[:, :, :], ALU.mult)
                take_o(l, 0, 0, 1)
                take_o(l, 1, 2, 2)
                head_norm(l, 0)
                dve.drain()
                dve.tensor_tensor(ONRM[:, :, T:2 * T], ONRM[:, :, T:2 * T], SIG[:, :, :],
                                  ALU.mult).then_inc(onrm_ready, 1)
                take_o(l, 2, 0, 3)
                heads_transposed(l, 0, 2)
                take_o(l, 3, 4, 4)
                heads_low(l, 0)
                dve.drain()
                dve.reciprocal(RDEN, OALL[:, :, 2 * GH:, HD])
                dve.drain()
                dve.tensor_tensor(OALL[:, :, 2 * GH:, 0:HD], OALL[:, :, 2 * GH:, 0:HD],
                                  RDEN.unsqueeze(3).to_broadcast([P, NTB, 2 * GH, HD]), ALU.mult).then_inc(o_scaled, 1)
                head_norm(l, 1).then_inc(onrm_ready, 1)
                heads_transposed(l, 1, 6)
                heads_low(l, 1)
                take_x(l * 2 + 1)
                norm(l * 2 + 1, side("g_ffn"))
                for b in range(NTB):
                    dve.wait_ge(score_read, l * 2 * NTB + 2 * b + 2)
                    dve.memset(GREC, 0.0)
                    for c in range(2 * HEADS):
                        dve.max(TOPV[:, c, 0:8], SCO[:, b, c, :])
                    dve.drain()
                    for c in range(2 * HEADS):
                        dve.max_index(TOPI[:, c, 0:8], TOPV[:, c, 0:8], SCO[:, b, c, :])
                        dve.match_replace(SCO2[:, c, :], TOPV[:, c, 0:8], SCO[:, b, c, :], LOWEST)
                    dve.drain()
                    for c in range(2 * HEADS):
                        dve.max(TOPV[:, c, 8:16], SCO2[:, c, :])
                    dve.drain()
                    for c in range(2 * HEADS):
                        dve.max_index(TOPI[:, c, 8:16], TOPV[:, c, 8:16], SCO2[:, c, :])
                    v = TOPV.rearrange("p (h c) k -> p h c k", c=2)
                    dve.tensor_tensor(CAND.rearrange("p h (a b) -> p h a b", a=TOPK),
                                      v[:, :, 0, :].unsqueeze(3).to_broadcast([P, HEADS, TOPK, TOPK]),
                                      v[:, :, 1, :].unsqueeze(2).to_broadcast([P, HEADS, TOPK, TOPK]), ALU.add)
                    dve.drain()
                    dve.tensor_copy(TOPF, TOPI.rearrange("p (h c) k -> p h c k", c=2))
                    for h in range(HEADS):
                        dve.max(BEST[:, h, 0:8], CAND[:, h, :])
                    dve.drain()
                    for h in range(HEADS):
                        dve.max_index(POS[:, h, 0:8], BEST[:, h, 0:8], CAND[:, h, :])
                        dve.match_replace(CAND2[:, h, :], BEST[:, h, 0:8], CAND[:, h, :], LOWEST)
                    dve.drain()
                    for h in range(HEADS):
                        dve.max(BEST[:, h, 8:16], CAND2[:, h, :])
                    dve.drain()
                    for h in range(HEADS):
                        dve.max_index(POS[:, h, 8:16], BEST[:, h, 8:16], CAND2[:, h, :])
                    last = dve.tensor_tensor(GSH[:, b], BEST, BEST[:, :, 0:1].to_broadcast([P, HEADS, TOPK]),
                                             ALU.subtract)
                    if b == NTB - 1:
                        last.then_inc(gate_shift, 1)
                    dve.drain()
                    dve.tensor_scalar(POSA[:, 0], POS, 4, None, ALU.logical_shift_right)
                    dve.tensor_scalar(POSA[:, 1], POS, TOPK - 1, None, ALU.bitwise_and)
                    dve.drain()
                    dve.tensor_copy(POSF, POSA)
                    dve.drain()
                    small_iota = iota[:, 0:TOPK].unsqueeze(1).to_broadcast([P, TOPK, TOPK]).unsqueeze(1)\
                        .to_broadcast([P, HEADS, TOPK, TOPK])
                    for c, pick in ((0, PICK), (1, PICK2)):
                        dve.tensor_tensor(pick, POSF[:, c].unsqueeze(3).to_broadcast([P, HEADS, TOPK, TOPK]),
                                          small_iota, ALU.is_equal)
                    dve.drain()
                    for c, pick in ((0, PICK), (1, PICK2)):
                        dve.tensor_tensor(pick, pick, TOPF[:, :, c, :].unsqueeze(2)
                                          .to_broadcast([P, HEADS, TOPK, TOPK]), ALU.mult)
                    dve.drain()
                    for c, pick in ((0, PICK), (1, PICK2)):
                        dve.tensor_reduce(CHOSEN[:, b, c, :].rearrange("p (h k) -> p h k", h=HEADS), pick, AX.X, ALU.add)
                dve.wait_ge(gate_exp, l + 1)
                dve.tensor_reduce(GSUM, GSH, AX.X, ALU.add)
                dve.drain()
                dve.reciprocal(GREC, GSUM)
                dve.drain()
                dve.tensor_tensor(CHOSEN[:, :, 2, :].rearrange("p b (h k) -> p b h k", h=HEADS), GSH,
                                  GREC.unsqueeze(3).to_broadcast([P, NTB, HEADS, TOPK]), ALU.mult).then_inc(chosen_ready, 1)
                for b in range(NTB):
                    dve.wait_ge(route_done, l * NTB + b + 1)
                    src = psum[:, 6 + b, 0:3 * P].rearrange("p (a t) -> p a t", a=3)
                    dve.tensor_copy(ROUTE[:, :, b * P:(b + 1) * P], src[:, 0:2, :])
                    last = dve.tensor_copy(GATE[:, b * P:(b + 1) * P], src[:, 2, :])
                last.then_inc(route_ready, 1)
                dve.drain()

                def onehot_rows(r, s, first=False):
                    if not first:
                        dve.wait_ge(onehot_i, l * GROUPS + r * 4 + s - 1)
                        dve.wait_ge(onehot_j, l * GROUPS + r * 4 + s - 1)
                    tok = ROUTE[:, :, bass.ds(r * 16 + s * 4, 4)].unsqueeze(2).to_broadcast([P, 2, NK, 4])
                    dve.tensor_tensor(OHB[s % 2], IOTA4.unsqueeze(1).to_broadcast([P, 2, NK, 4]), tok,
                                      ALU.is_equal).then_inc(onehot_equal, 1)

                def early_weights(r, s):
                    dve.wait_ge(gate_copied, l * GROUPS + r * 4 + s + 1)
                    cols = G[:, 0:EARLY, bass.ds(r * 16 + s * 4, 4)]
                    dve.tensor_tensor(cols, psum[:, 4 + s, :].rearrange("p (t j) -> p j t", t=4)[:, 0:EARLY, :],
                                      cols, ALU.mult).then_inc(gate_read, 1)

                dve.wait_ge(resid_in, l + 1)
                onehot_rows(0, 0, True)
                onehot_rows(0, 1, True)
                for m in range(2):
                    low(l, M_DENSE + m)
                onehot_rows(0, 2)
                onehot_rows(0, 3)
                with dve.Fori(0, GROUPS // 4 - 1) as r:
                    for s in range(4):
                        onehot_rows(r, s + 4)
                        early_weights(r, s)
                for s in range(4):
                    early_weights(GROUPS // 4 - 1, s)
                dve.drain()

                def weigh(col, a, used, gelu):
                    wj = G[:, bass.ds(col, 1), :]
                    if gelu is not None:
                        dve.wait_ge(gelu_ready, l * LATE + gelu)
                        dve.tensor_tensor(wj, GEL[:, a, :].unsqueeze(1), wj, ALU.mult)
                        dve.drain()
                    dve.wait_ge(card_used, l * CARDS + used)
                    dve.tensor_scalar(WH[:, a, :].unsqueeze(1), wj, 1.0, None, ALU.mult)
                    dve.drain()
                    dve.tensor_tensor(WL[:, a, :].unsqueeze(1), wj, WH[:, a, :].bitcast(F32).unsqueeze(1),
                                      ALU.subtract).then_inc(wt_ready, 1)

                with dve.Fori(0, EARLY // 4) as r:
                    for s in range(4):
                        weigh(r * 4 + s, s % 2, M_FIRST + s + r * 4, None)
                        low(l, M_DENSE + 2 + s, r)
                low(l, M_STEP + 1)
                weigh(EARLY, 0, M_STEP - 1, 1)
                with dve.Fori(0, STEP_PAIRS) as r:
                    for s in range(2):
                        low(l, M_STEP + 2 + 2 * s, r)
                        low(l, M_STEP + 3 + 2 * s, r)
                        weigh(r * 2 + EARLY + s + 1, (s + 1) % 2, M_STEP + 2 * s + r * 4, r * 2 + s + 2)
                low(l, CARDS - 1)
                weigh(NK - 1, 1, CARDS - 3, LATE)
                take_x(l * 2 + 2)
            norm_rstd(DEPTH * 2)
            dve.wait_ge(x_last, DEPTH * 2 + 1)
            dve.wait_ge(side_loaded, DEPTH * 16 + 16)
            for b in range(NTB):
                dve.scalar_tensor_tensor(XN[:, b, :], X[:, b, :], RSTD[:, b:b + 1], GFIN, ALU.mult, ALU.mult)\
                    .then_inc(y_ready, 1)

        @block.tensor
        def _(pe):
            def card(l, m, r=0):
                if m < M_DENSE:
                    pe.wait_ge(pool_split, l * M_DENSE + m + 1 + SLOTS * r)
                else:
                    pe.wait_ge(split_ready, SLOTS + l * SPLITS + m - M_DENSE + 1 + SLOTS * r)
                return CH_[:, m % SLOTS, :], CL_[:, m % SLOTS, :]

            def product(out, wh, wl, xh, xl, start, stop):
                pe.matmul(out, wh, xh, start=start, stop=False)
                pe.matmul(out, wh, xl, start=False, stop=False)
                return pe.matmul(out, wl, xh, start=False, stop=stop)

            def residual(n):
                return pe.matmul(psum[:, n, :], ident, X[:, n // 2, (n % 2) * 512:(n % 2 + 1) * 512],
                                 start=True, stop=False)

            def flip_norm(n, meanwhile=()):
                for m in range(4):
                    q, b = m // 2, m % 2
                    if m < 2:
                        pe.wait_ge(x_taken, n * 3 + 2 * b + 1)
                    elif m == 3:
                        pe.wait_ge(x_last, n + 1)
                    for k in range(4):
                        last = pe.transpose(psum[:, 4 + m, k * P:(k + 1) * P],
                                            X[:, b, (4 * q + k) * P:(4 * q + k + 1) * P], ident)
                    last.then_inc(xt_done, 1)
                for quarter in meanwhile:
                    residual(quarter)
                pe.wait_ge(diag_ready, n + 1)
                for b in range(NTB):
                    last = pe.matmul(psum[:, 3, b * P:(b + 1) * P], ONES, DIAG[:, b, :], start=True, stop=True)
                last.then_inc(rstd_spread, 1)

            def columns_first(l, m, bank, r=0, norm=None):
                wh, wl = [w.rearrange("p (k c) -> p k c", k=KT) for w in card(l, m, r)]
                for k in range(KT):
                    if norm is not None and k % 2 == 0:
                        pe.wait_ge(h_low, norm * 4 + k // 2 + 1)
                    last = product(psum[:, bank, 0:T], wh[:, k, :], wl[:, k, :], HTH[:, k, :], HTL[:, k, :],
                                   k == 0, k == KT - 1)
                last.then_inc(card_used, 1)

            def pv(g, bank):
                for b in range(NTB):
                    for h in range(GH):
                        o = psum[:, bank + b, h * HV:(h + 1) * HV]
                        if b == 0:
                            last = pe.matmul(o, PT[g][:, h, 0:P], VN[:, 0, GH * g + h, :], start=True, stop=True)
                        else:
                            pe.matmul(o, PT[g][:, h, P:2 * P], VN[:, 0, GH * g + h, :], start=True, stop=False)
                            last = pe.matmul(o, PT[g][:, h, 2 * P:KQ], VN[:, 1, GH * g + h, :], start=False, stop=True)
                last.then_inc(pv_done, 1)

            def qk_scores(q, k, bank):
                for h in range(GH):
                    rows = slice(HD * (h % 2), HD * (h % 2) + HD)
                    qT, kT = QK[rows, q + h // 2, :], QK[rows, k + h // 2, :]
                    pe.matmul(psum[:, bank + h, 0:P], qT[:, 0:P], kT[:, 0:P], start=True, stop=True)
                    last = pe.matmul(psum[:, bank + h, P:KQ], qT[:, P:T], kT[:, 0:T], start=True, stop=True)
                return last

            def flip(src, bank):
                for h in range(GH):
                    for n in range(3):
                        last = pe.transpose(psum[:, bank + h, n * P:(n + 1) * P], src[:, h, n * P:(n + 1) * P], ident)
                return last

            pe.wait_ge(start_loaded, 16)
            pe.wait_ge(x_loaded, 16)
            with pe.Fori(0, DEPTH) as l:
                flip_norm(l * 2)
                pe.wait_ge(side_loaded, l * 16 + 16)
                for k in range(KT):
                    if k % 4 == 0:
                        pe.wait_ge(ht_ready, l * 2 * KT + k + 4)
                    last = pe.matmul(psum[0:SMALL, 0, 0:T], wsmall[:, k, :], HT[:, k, :],
                                     start=(k == 0), stop=(k == KT - 1))
                last.then_inc(small_done, 1)
                for c in range(C_IN):
                    if c == 2:
                        pe.wait_ge(gd_ready, l + 1)
                        pe.matmul(psum[:, 1, 0:T], side("up")[0:RANK, :], GDT[0:RANK, :],
                                  start=True, stop=True).then_inc(gl_done, 1)
                    if c < IN_T:
                        if c >= 4:
                            pe.wait_ge(proj_read, l * (IN_T + 5) + c - 3)
                        columns_first(l, c, 4 + c % 4, norm=None if c else l * 2)
                    else:
                        p, half = (c - IN_T) // 2, (c - IN_T) % 2
                        if half == 0:
                            pe.wait_ge(proj_read, l * (IN_T + 5) + (12, 14, 15, 16, 17)[p])
                        wh, wl = [w.rearrange("p (k c) -> p k c", k=4) for w in card(l, c)]
                        for b in range(NTB):
                            for k in range(4):
                                kk, tb = 4 * half + k, slice(b * P, (b + 1) * P)
                                last = product(psum[:, v_bank(p) + b, 0:T], HTH[:, kk, tb], HTL[:, kk, tb],
                                               wh[:, k, :], wl[:, k, :], kk == 0, kk == KT - 1)
                        last.then_inc(card_used, 1)
                    if c == AFTER["a_scores"]:
                        pe.wait_ge(gly_ready, l + 1)
                        pe.wait_ge(proj_read, l * (IN_T + 5) + 4)
                        for h in range(GH):
                            rows = slice(HD * (h % 2), HD * (h % 2) + HD)
                            qT, kT = QK[rows, AQ + h // 2, :], QK[rows, AK + h // 2, :]
                            pe.matmul(psum[:, h, 0:T], kT[:, 0:P], qT[:, 0:T], start=True, stop=True)
                            last = pe.matmul(psum[:, h, T:KQ], kT[:, P:T], qT[:, P:T], start=True, stop=True)
                        last.then_inc(a_scores, 1)
                    if c == AFTER["a_tail"]:
                        pe.wait_ge(a_sp, l + 1)
                        for h in range(GH):
                            pe.matmul(psum[:, h, 0:T], mc("tri"), SA[:, h, 0:T], start=True, stop=False)
                            pe.matmul(psum[:, h, P:T], mc("ones")[:, 0:P], SA[:, h, T:KQ], start=False, stop=True)
                            last = pe.matmul(psum[:, h, T:KQ], mc("tri"), SA[:, h, T:KQ], start=True, stop=True)
                        last.then_inc(a_tail, 1)
                    if c == AFTER["b_scores"]:
                        pe.wait_ge(a_logw, l + 1)
                        pe.wait_ge(glq_ready, l + 1)
                        for n in reversed(range(NCH)):
                            for kb in range(n // 4 + 1):
                                m = P if kb < n // 4 else CH * (n % 4 + 1)
                                col = P * (n % 4)
                                last = pe.matmul(psum[0:m, n // 4 + kb, col:col + P],
                                                 KDEC[:, CHOFF[n] + kb * P:CHOFF[n] + kb * P + m],
                                                 GLQD[:, n, :, :], start=True, stop=True)
                        last.then_inc(b_scores, 1)
                    if c == AFTER["c_scores"]:
                        pe.wait_ge(b_ready, l + 1)
                        qk_scores(CQ, CK, 0).then_inc(c_scores, 1)
                    if c == AFTER["fox_gates"]:
                        pe.wait_ge(foxc_ready, l + 1)
                        pe.wait_ge(c_read, l + 1)
                        for h in range(GH):
                            last = pe.matmul(psum[:, h, 0:T], mc("head_sel")[FOX0:SMALL, h * P:(h + 1) * P],
                                             FOXC[FOX0:SMALL, :], start=True, stop=True)
                        last.then_inc(foxb_done, 1)
                    if c == AFTER["d_scores"]:
                        pe.wait_ge(foxb_read, l + 1)
                        pe.wait_ge(proj_read, l * (IN_T + 5) + IN_T)
                        qk_scores(DQ, DKEY, 0).then_inc(d_scores, 1)
                    if c == AFTER["c_flip"]:
                        pe.wait_ge(d_read, l + 1)
                        pe.wait_ge(c_prob, l + 1)
                        flip(SC, 0).then_inc(c_flip, 1)
                    if c == AFTER["d_flip"]:
                        pe.wait_ge(c_ready, l + 1)
                        pe.wait_ge(d_exp, l + 1)
                        flip(SD, 0).then_inc(d_flip, 1)
                    if c == AFTER["ab_out"]:
                        pe.wait_ge(d_ready, l + 1)
                        pe.wait_ge(a_ready, l + 1)
                        pe.wait_ge(proj_read, l * (IN_T + 5) + IN_T + 3)
                        pv(0, 0)
                        pv(1, 2)
                    if c == AFTER["c_out"]:
                        pe.wait_ge(o_ready, l * 4 + 1)
                        pe.wait_ge(proj_read, l * (IN_T + 5) + IN_T + 4)
                        pv(2, 0)
                def heads_flip(q, bank):
                    pe.wait_ge(onrm_ready, l * 2 + q + 1)
                    for b in range(NTB):
                        for k in range(4):
                            last = pe.transpose(psum[:, bank + b, k * P:(k + 1) * P],
                                                ONRM[:, b, (4 * q + k) * P:(4 * q + k + 1) * P], ident)
                        last.then_inc(ot_done, 1)

                heads_flip(0, 2)
                pe.wait_ge(proj_read, l * (IN_T + 5) + IN_T + 5)
                pv(3, 4)

                pe.wait_ge(o_ready, l * 4 + 3)
                pe.wait_ge(ot_ready, l * 4 + 2)
                for n in range(4):
                    residual(n)

                def rows_first(m, ah, al, stop, r=0):
                    ch, cl = card(l, m, r)
                    for n in range(4):
                        if stop and n:
                            last.then_inc(x_sum, 1)
                        tb, half = slice((n // 2) * P, (n // 2 + 1) * P), slice((n % 2) * 512, (n % 2 + 1) * 512)
                        last = product(psum[:, n, :], ah[:, tb], al[:, tb], ch[:, half], cl[:, half], False, stop)
                    last.then_inc(card_used, 1)

                for k in range(C_OUT):
                    if k % 4 == 0:
                        pe.wait_ge(o_low, l * 2 + k // 4 + 1)
                    if k == 3:
                        heads_flip(1, 6)
                    rows_first(M_OUT + k, HTH[:, k, :], HTL[:, k, :], k == C_OUT - 1)
                flip_norm(l * 2 + 1, meanwhile=(0, 1))
                for n in (2, 3):
                    if n == 3:
                        pe.wait_ge(ht_ready, l * 2 * KT + KT + 1)
                    last = residual(n)
                last.then_inc(resid_in, 1)
                for c in range(C_PQ):
                    if c >= 4:
                        pe.wait_ge(pq_read, l * C_PQ + c - 3)
                    columns_first(l, M_PQ + c, 4 + c % 4, norm=None if c else l * 2 + 1)
                pe.wait_ge(pq_read, l * C_PQ + C_PQ)
                for b in range(NTB):
                    for c in range(2 * HEADS):
                        if b and c % 8 == 0:
                            pe.wait_ge(score_read, l * 2 * NTB + c // 8 + 1)
                        last = pe.matmul(psum[:, 4 + c // 4, (c % 4) * NK:(c % 4 + 1) * NK],
                                         QRY[:, c, b * P:(b + 1) * P], subk[:, c, :], start=True, stop=True)
                        if c % 8 == 7:
                            last.then_inc(score_done, 1)
                pe.wait_ge(score_read, l * 2 * NTB + 2 * NTB - 1)
                def choices_flip():
                    pe.wait_ge(chosen_ready, l + 1)
                    for b in range(NTB):
                        for a in range(3):
                            last = pe.transpose(psum[:, 6 + b, a * P:(a + 1) * P], CHOSEN[:, b, a, :], ident)
                        last.then_inc(route_done, 1)

                def early_columns(r, first, flip_at=None):
                    for s in range(4):
                        if s == flip_at:
                            choices_flip()
                        if s >= 2 or not first:
                            pe.wait_ge(early_read, l * EARLY + r * 4 + s - 1)
                        columns_first(l, M_EARLY + s, 4 + s % 2, r)

                early_columns(0, True)
                with pe.Fori(1, EARLY // 4 - 1) as r:
                    early_columns(r, False)
                early_columns(EARLY // 4 - 1, False, flip_at=2)
                pe.wait_ge(route_ready, l + 1)
                pe.wait_ge(start_loaded, 16)
                def gate_groups(r, first):
                    for s in range(4):
                        pe.wait_ge(onehot_i, l * GROUPS + r * 4 + s + 1)
                        pe.wait_ge(onehot_j, l * GROUPS + r * 4 + s + 1)
                        if not first:
                            pe.wait_ge(gate_read, l * GROUPS + r * 4 + s - 3)
                        for t in range(4):
                            last = pe.matmul(psum[:, 4 + s, t * NK:(t + 1) * NK], OH[s][:, 0, t, :], OH[s][:, 1, t, :],
                                             start=True, stop=True)
                        last.then_inc(gate_done, 1)

                gate_groups(0, True)
                with pe.Fori(1, GROUPS // 4) as r:
                    gate_groups(r, False)
                pe.wait_ge(gate_read, l * GROUPS + GROUPS - 3)
                columns_first(l, M_FIRST, 4)
                with pe.Fori(0, EARLY // 4) as r:
                    for s in range(4):
                        pe.wait_ge(wt_ready, l * NK + r * 4 + s + 1)
                        rows_first(M_FIRST + 1 + s, WH[:, s % 2, :], WL[:, s % 2, :], False, r)

                def step(r, s, stop):
                    columns_first(l, M_STEP + 2 * s, 4 + (s + 1) % 2, r)
                    pe.wait_ge(wt_ready, l * NK + EARLY + r * 2 + s + 1)
                    rows_first(M_STEP + 1 + 2 * s, WH[:, s % 2, :], WL[:, s % 2, :], stop, r)

                with pe.Fori(0, STEP_PAIRS) as r:
                    for s in range(2):
                        step(r, s, False)
                step(STEP_PAIRS, 0, False)
                pe.wait_ge(wt_ready, (l + 1) * NK)
                rows_first(CARDS - 1, WH[:, 1, :], WL[:, 1, :], True)


def kernel(x, norm_mix_g, w_in, w_gla_up, b_gla, b_fox, head_norm_g, w_out, norm_ffn_g,
           w_peer_q, peer_sub_keys, peer_u, peer_v, norm_final_g):
    import concourse.bacc as bacc
    from concourse.bass_utils import run_bass_kernel_spmd

    f32 = np.float32
    w_in, w_out, w_peer_q = np.asarray(w_in), np.asarray(w_out), np.asarray(w_peer_q)
    peer_u, peer_v = np.asarray(peer_u), np.asarray(peer_v)

    def columns(w):
        return w.reshape(KT, P, -1, P).transpose(2, 1, 0, 3).reshape(-1, P, CF)

    def halves(w):
        return w.reshape(2, KT // 2, P, -1, 256).transpose(3, 0, 2, 1, 4).reshape(-1, P, CF)

    widths = (256, 256, 256, 128, 128, 256, 256, 16, 256, 256, 256, 256, 256, 256, 4)
    ends = np.cumsum(widths)
    part = [slice(e - w, e) for e, w in zip(ends, widths)]
    by_column, by_token = [0, 1, 3, 4, 8, 9, 11, 12], [6, 2, 5, 10, 13]

    u_at = np.array([M_EARLY + j for j in range(EARLY + 1)] + [M_STEP + 2 * n for n in range(LATE - 1)])
    v_at = np.array([M_FIRST + 1 + j for j in range(EARLY)] + [M_STEP + 1 + 2 * n for n in range(LATE - 1)]
                    + [CARDS - 1])

    stream = np.empty((DEPTH, CARDS, P, CF), f32)
    sides = np.zeros((DEPTH + 1, P, SIDE_F), f32)
    sides[DEPTH, :, 0:D] = np.asarray(norm_final_g)
    for l in range(DEPTH):
        stream[l, 0:IN_T] = columns(np.concatenate([w_in[l][:, part[n]] for n in by_column], 1))
        stream[l, IN_T:C_IN] = halves(np.concatenate([w_in[l][:, part[n]] for n in by_token], 1))
        stream[l, M_OUT:M_PQ] = w_out[l].reshape(C_OUT, P, CF)
        stream[l, M_PQ:M_EARLY] = columns(w_peer_q[l])
        stream[l, u_at] = peer_u[l].reshape(P, NK, KT, P).transpose(1, 3, 2, 0).reshape(NK, P, CF)
        stream[l, v_at] = peer_v[l].reshape(P, NK, D).transpose(1, 0, 2)

        def put(name, a):
            s, e = SIDE[name]
            sides[l, :a.shape[0], s:e] = a.reshape(a.shape[0], -1)

        put("subk", np.asarray(peer_sub_keys)[l].transpose(3, 0, 1, 2))
        small = np.zeros((P, KT, SMALL), f32)
        small[:, :, 0:RANK] = w_in[l][:, part[7]].reshape(KT, P, RANK).transpose(1, 0, 2)
        small[:, :, FOX0:] = w_in[l][:, part[14]].reshape(KT, P, GH).transpose(1, 0, 2)
        put("small", small)
        put("up", np.asarray(w_gla_up)[l])
        put("b_gla", np.asarray(b_gla)[l][:, None])
        sides[l, FOX0:SMALL, SIDE["b_fox"][0]] = np.asarray(b_fox)[l]
        put("g_mix", np.asarray(norm_mix_g)[l].reshape(KT, P).T)
        put("g_head", np.asarray(head_norm_g)[l].reshape(KT, P).T)
        put("g_ffn", np.asarray(norm_ffn_g)[l].reshape(KT, P).T)

    mixc, fixed = host_constants()
    arrays = {
        "x_in": np.ascontiguousarray(x),
        "stream": stream.reshape(DEPTH * CARDS, P, CF),
        "side": sides,
        "mixc": mixc,
        "fixed": fixed,
    }
    nc = bacc.Bacc("TRN2", target_bir_lowering=False, num_devices=1, dynamic_dma_scratch_size=1024)
    aps = [nc.dram_tensor(n, a.shape, F32, kind="ExternalInput").ap() for n, a in arrays.items()]
    y = nc.dram_tensor("y", (1, T, D), F32, kind="ExternalOutput").ap()
    build(nc, *aps, y)
    r = run_bass_kernel_spmd(nc, [arrays], core_ids=[0])
    return r.results[0]["y"]
```
